# Optimizing a Trainium2 kernel written in Bass

```python
import jax, jax.numpy as jnp
from jax import lax
import numpy as np

D_MODEL = 1024
BATCH = 1
SEQ = 512
DEPTH = 2
DEC_BATCH = 1
DEC_SEQ = 64
PAST_LEN = 128

CHUNK = 64
N_MIXERS = 2
N_POOL_LAYERS = (DEPTH + 1) // N_MIXERS
N_MLSTM_LAYERS = DEPTH // N_MIXERS
POOL_WINDOWS = (2, 4, 8, 16)
POOL_GROUPS = len(POOL_WINDOWS)
POOL_GROUP_WIDTH = D_MODEL // POOL_GROUPS
POOL_HIST = max(POOL_WINDOWS) - 1
MLSTM_HEADS = 4
MLSTM_DQK = D_MODEL // (2 * MLSTM_HEADS)
MLSTM_DV = D_MODEL // MLSTM_HEADS
MLSTM_QK = MLSTM_HEADS * MLSTM_DQK
MLSTM_V = MLSTM_HEADS * MLSTM_DV
MLSTM_IN = 2 * MLSTM_QK + 2 * MLSTM_V + 2 * MLSTM_HEADS
D_FF = 2816
EPS = 1e-6

kernel_name = 'pool_mlstm_macaron_stream_step'

def _rmsnorm(x, g):
    x32 = x.astype(jnp.float32)
    y = x32 * lax.rsqrt(jnp.mean(x32 * x32, axis=-1, keepdims=True) + EPS) * g.astype(jnp.float32)
    return y.astype(x.dtype)

def _swiglu(u, w_in, w_out):
    h = u @ w_in
    a, b = h[..., :D_FF], h[..., D_FF:]
    return (jax.nn.silu(a) * b) @ w_out

def _pool_mixer(u, hist, pos0, w_pool, b_pool, scale):
    B, S, _ = u.shape
    ext = jnp.concatenate([hist.astype(u.dtype), u], axis=1)
    ext32 = ext.astype(jnp.float32)
    csum = jnp.pad(jnp.cumsum(ext32, axis=1), ((0, 0), (1, 0), (0, 0)))
    pos = pos0 + jnp.arange(S)
    hi = csum[:, POOL_HIST + 1:POOL_HIST + 1 + S]
    means = []
    for g, w in enumerate(POOL_WINDOWS):
        c = slice(g * POOL_GROUP_WIDTH, (g + 1) * POOL_GROUP_WIDTH)
        lo = csum[:, POOL_HIST + 1 - w:POOL_HIST + 1 - w + S, c]
        cnt = jnp.minimum(pos + 1, w).astype(jnp.float32)
        means.append((hi[..., c] - lo) / cnt[None, :, None])
    d = jnp.concatenate(means, axis=-1) - ext32[:, POOL_HIST:]
    d = d.reshape(B, S, POOL_GROUPS, POOL_GROUP_WIDTH)
    y = jnp.einsum('bsgc,gce->bsge', d, w_pool.astype(jnp.float32)).reshape(B, S, D_MODEL)
    y = (y + b_pool.astype(jnp.float32)) * scale.astype(jnp.float32)
    return y.astype(u.dtype), ext[:, -POOL_HIST:]

def _mlstm_cell(q, k, v, log_i, log_f, C0, n0, m0):
    B, S, H, _ = q.shape
    L = min(CHUNK, S)
    NC = S // L

    def blocks(a):
        a = a.reshape((B, NC, L, H) + a.shape[3:])
        return jnp.moveaxis(a, (1, 3), (0, 2))

    causal = jnp.tril(jnp.ones((L, L), dtype=bool))

    def step(carry, xs):
        C, n, m = carry
        qc, kc, vc, ic, fc = xs
        b = jnp.cumsum(fc, axis=-1)
        log_d = jnp.where(causal, b[..., :, None] - b[..., None, :] + ic[..., None, :], -jnp.inf)
        log_state = b + m[..., None]
        m_t = jnp.maximum(jnp.max(log_d, axis=-1), log_state)
        w_intra = jnp.exp(log_d - m_t[..., None])
        w_state = jnp.exp(log_state - m_t)
        s = jnp.einsum('bhtd,bhsd->bhts', qc, kc) * w_intra
        num = jnp.einsum('bhts,bhsv->bhtv', s, vc) + w_state[..., None] * jnp.einsum('bhvd,bhtd->bhtv', C, qc)
        den = jnp.sum(s, axis=-1) + w_state * jnp.einsum('bhd,bhtd->bht', n, qc)
        h = num / jnp.maximum(jnp.abs(den), jnp.exp(-m_t))[..., None]
        m_new = m_t[..., -1]
        w_carry = jnp.exp(b[..., -1] + m - m_new)
        w_write = jnp.exp(b[..., -1:] - b + ic - m_new[..., None])
        C_new = w_carry[..., None, None] * C + jnp.einsum('bhsv,bhsd->bhvd', vc * w_write[..., None], kc)
        n_new = w_carry[..., None] * n + jnp.einsum('bhs,bhsd->bhd', w_write, kc)
        return (C_new, n_new, m_new), h

    init = (C0.astype(jnp.float32), n0.astype(jnp.float32), m0.astype(jnp.float32))
    xs = (blocks(q), blocks(k), blocks(v), blocks(log_i), blocks(log_f))
    (C, n, m), h = lax.scan(step, init, xs)
    h = jnp.moveaxis(h, (0, 2), (1, 3)).reshape(B, S, H, MLSTM_DV)
    return h, (C, n, m)

def _mlstm_mixer(u, C0, n0, m0, w_in, b_i, b_f, g_norm, w_out):
    B, S, _ = u.shape
    p = u @ w_in
    o0 = 2 * MLSTM_QK + MLSTM_V
    g0 = o0 + MLSTM_V
    q = p[..., :MLSTM_QK].astype(jnp.float32).reshape(B, S, MLSTM_HEADS, MLSTM_DQK) * (MLSTM_DQK ** -0.5)
    k = p[..., MLSTM_QK:2 * MLSTM_QK].astype(jnp.float32).reshape(B, S, MLSTM_HEADS, MLSTM_DQK)
    v = p[..., 2 * MLSTM_QK:o0].astype(jnp.float32).reshape(B, S, MLSTM_HEADS, MLSTM_DV)
    o = p[..., o0:g0].astype(jnp.float32)
    log_i = p[..., g0:g0 + MLSTM_HEADS].astype(jnp.float32) + b_i.astype(jnp.float32)
    log_f = jax.nn.log_sigmoid(p[..., g0 + MLSTM_HEADS:].astype(jnp.float32) + b_f.astype(jnp.float32))
    h, state = _mlstm_cell(q, k, v, log_i, log_f, C0, n0, m0)
    h = h * lax.rsqrt(jnp.mean(h * h, axis=-1, keepdims=True) + EPS)
    h = h.reshape(B, S, MLSTM_V) * g_norm.astype(jnp.float32)
    y = (jax.nn.sigmoid(o) * h).astype(u.dtype) @ w_out
    return y, state

def _trunk(x, pool_hist, mC, mn, mm, pos0, norm_ffn1, ffn1_w_in, ffn1_w_out, norm_mix, pool_w, pool_b,
           pool_scale, mlstm_w_in, mlstm_b_i, mlstm_b_f, mlstm_norm, mlstm_w_out, norm_ffn2, ffn2_w_in,
           ffn2_w_out, norm_final):
    pool_new, C_new, n_new, m_new = [], [], [], []
    for i in range(DEPTH):
        j = i // N_MIXERS
        x = x + 0.5 * _swiglu(_rmsnorm(x, norm_ffn1[i]), ffn1_w_in[i], ffn1_w_out[i])
        u = _rmsnorm(x, norm_mix[i])
        if i % N_MIXERS == 0:
            y, hist = _pool_mixer(u, pool_hist[j], pos0, pool_w[j], pool_b[j], pool_scale[j])
            pool_new.append(hist.astype(pool_hist.dtype))
        else:
            y, (C, n, m) = _mlstm_mixer(u, mC[j], mn[j], mm[j], mlstm_w_in[j], mlstm_b_i[j], mlstm_b_f[j],
                                        mlstm_norm[j], mlstm_w_out[j])
            C_new.append(C.astype(mC.dtype))
            n_new.append(n.astype(mn.dtype))
            m_new.append(m.astype(mm.dtype))
        x = x + y
        x = x + 0.5 * _swiglu(_rmsnorm(x, norm_ffn2[i]), ffn2_w_in[i], ffn2_w_out[i])
    return _rmsnorm(x, norm_final), jnp.stack(pool_new), jnp.stack(C_new), jnp.stack(n_new), jnp.stack(m_new)

def setup_inputs(seed: int = 0) -> dict:
    key = jax.random.key(seed)
    ks = jax.random.split(key, 24)
    f32 = jnp.float32

    def nrm(k, shape, scale):
        return jax.random.normal(k, shape, f32) * scale

    b_f = jnp.broadcast_to(jnp.linspace(3.0, 6.0, MLSTM_HEADS, dtype=f32), (N_MLSTM_LAYERS, MLSTM_HEADS))
    return {
        'x_prompt': nrm(ks[0], (BATCH, SEQ, D_MODEL), 1.0),
        'x_sample': nrm(ks[1], (DEC_BATCH, DEC_SEQ, D_MODEL), 1.0),
        'state_pool': nrm(ks[2], (N_POOL_LAYERS, DEC_BATCH, POOL_HIST, D_MODEL), 1.0),
        'state_mlstm_C': nrm(ks[3], (N_MLSTM_LAYERS, DEC_BATCH, MLSTM_HEADS, MLSTM_DV, MLSTM_DQK), 0.1),
        'state_mlstm_n': nrm(ks[4], (N_MLSTM_LAYERS, DEC_BATCH, MLSTM_HEADS, MLSTM_DQK), 0.1),
        'state_mlstm_m': nrm(ks[5], (N_MLSTM_LAYERS, DEC_BATCH, MLSTM_HEADS), 0.5),
        'norm_ffn1': 1.0 + nrm(ks[6], (DEPTH, D_MODEL), 0.05),
        'ffn1_w_in': nrm(ks[7], (DEPTH, D_MODEL, 2 * D_FF), D_MODEL ** -0.5),
        'ffn1_w_out': nrm(ks[8], (DEPTH, D_FF, D_MODEL), D_FF ** -0.5),
        'norm_mix': 1.0 + nrm(ks[9], (DEPTH, D_MODEL), 0.05),
        'pool_w': nrm(ks[10], (N_POOL_LAYERS, POOL_GROUPS, POOL_GROUP_WIDTH, POOL_GROUP_WIDTH), POOL_GROUP_WIDTH ** -0.5),
        'pool_b': nrm(ks[11], (N_POOL_LAYERS, D_MODEL), 0.02),
        'pool_scale': 1.0 + nrm(ks[12], (N_POOL_LAYERS, D_MODEL), 0.1),
        'mlstm_w_in': nrm(ks[13], (N_MLSTM_LAYERS, D_MODEL, MLSTM_IN), D_MODEL ** -0.5),
        'mlstm_b_i': nrm(ks[14], (N_MLSTM_LAYERS, MLSTM_HEADS), 0.1),
        'mlstm_b_f': b_f + nrm(ks[15], (N_MLSTM_LAYERS, MLSTM_HEADS), 0.1),
        'mlstm_norm': 1.0 + nrm(ks[16], (N_MLSTM_LAYERS, MLSTM_V), 0.05),
        'mlstm_w_out': nrm(ks[17], (N_MLSTM_LAYERS, MLSTM_V, D_MODEL), MLSTM_V ** -0.5),
        'norm_ffn2': 1.0 + nrm(ks[18], (DEPTH, D_MODEL), 0.05),
        'ffn2_w_in': nrm(ks[19], (DEPTH, D_MODEL, 2 * D_FF), D_MODEL ** -0.5),
        'ffn2_w_out': nrm(ks[20], (DEPTH, D_FF, D_MODEL), D_FF ** -0.5),
        'norm_final': 1.0 + nrm(ks[21], (D_MODEL,), 0.05),
    }

def reference(x_prompt, x_sample, state_pool, state_mlstm_C, state_mlstm_n, state_mlstm_m, norm_ffn1,
              ffn1_w_in, ffn1_w_out, norm_mix, pool_w, pool_b, pool_scale, mlstm_w_in, mlstm_b_i, mlstm_b_f,
              mlstm_norm, mlstm_w_out, norm_ffn2, ffn2_w_in, ffn2_w_out, norm_final):
    weights = (norm_ffn1, ffn1_w_in, ffn1_w_out, norm_mix, pool_w, pool_b, pool_scale, mlstm_w_in, mlstm_b_i,
               mlstm_b_f, mlstm_norm, mlstm_w_out, norm_ffn2, ffn2_w_in, ffn2_w_out, norm_final)
    B = x_prompt.shape[0]
    zero_pool = jnp.zeros((N_POOL_LAYERS, B, POOL_HIST, D_MODEL), state_pool.dtype)
    zero_C = jnp.zeros((N_MLSTM_LAYERS, B, MLSTM_HEADS, MLSTM_DV, MLSTM_DQK), state_mlstm_C.dtype)
    zero_n = jnp.zeros((N_MLSTM_LAYERS, B, MLSTM_HEADS, MLSTM_DQK), state_mlstm_n.dtype)
    zero_m = jnp.zeros((N_MLSTM_LAYERS, B, MLSTM_HEADS), state_mlstm_m.dtype)
    y_prompt, pool_p, C_p, n_p, m_p = _trunk(x_prompt, zero_pool, zero_C, zero_n, zero_m, 0, *weights)
    y_sample, pool_s, C_s, n_s, m_s = _trunk(x_sample, state_pool, state_mlstm_C, state_mlstm_n,
                                             state_mlstm_m, PAST_LEN, *weights)
    return (y_prompt, y_sample, pool_p, C_p, n_p, m_p, pool_s, C_s, n_s, m_s)


_drawn_inputs = setup_inputs


def setup_inputs(seed=0):
    import zlib

    import numpy as np

    out = dict(_drawn_inputs(seed))
    spreads = {}
    factors = {'state_mlstm_n': 8.0, 'state_mlstm_m': 8.0, 'mlstm_norm': 3.12}
    for name, (base, spread) in spreads.items():
        noise = np.random.default_rng([zlib.crc32(name.encode()), seed]).standard_normal(out[name].shape)
        drawn = base * np.exp(spread * noise) if base else spread * noise
        out[name] = __import__('jax').numpy.asarray(drawn.astype(out[name].dtype))
    for name, factor in factors.items():
        out[name] = (out[name] * factor).astype(out[name].dtype)
    return out
```

```python
import concourse.bass as bass
from concourse import mybir

P = 128
D_MODEL = 1024
DT = D_MODEL // P
SEQ, DEC_SEQ = 512, 64
TOK = SEQ + DEC_SEQ
HALF = TOK // 2
D_FF = 2816
FT = D_FF // P
HIST = 15
GROUPS = 4
EXT = TOK + 2 * HIST
PROMPT0, SAMPLE0 = HIST, HIST + SEQ + HIST
HEADS = 4
DV = 256
CH = 128
NB = SEQ // CH + 1
EPS = 1e-6
RING, RAW = 4, 2

U_IN, U_OUT = 2 * FT, 3 * DT
FFN_UNITS = U_IN + U_OUT
U_A = 0
U_POOL = U_A + FFN_UNITS
U_B = U_POOL + GROUPS
U_C = U_B + FFN_UNITS
U_M = U_C + FFN_UNITS
N_PROJ = 3 * DT
U_MOUT = U_M + 1 + N_PROJ
U_D = U_MOUT + DT
U_END = U_D + FFN_UNITS
OUT_UNIT = (8, 8, 6)


def unit_blocks(n):
    for start in (U_A, U_B, U_C, U_D):
        if start + U_IN <= n < start + FFN_UNITS:
            return OUT_UNIT[(n - start - U_IN) % 3]
    if U_POOL <= n < U_B:
        return 4
    return 8


def encoder_step(nc, a):
    F32, F32R = mybir.dt.float32, mybir.dt.float32r
    ALU, ACT = mybir.AluOpType, mybir.ActivationFunctionType

    place = [(nc.sbuf_base + 63) // 64 * 64]

    def sb(name, shape, dt=F32, at=None):
        size = 4
        for s in shape[1:]:
            size *= s
        offset = place[0] if at is None else at
        if at is None:
            place[0] += (size + 31) // 32 * 32
        return nc.alloc_sbuf_tensor_at(name, shape, dt, offset=offset)

    x = sb("x", [P, DT, TOK])
    u_hi, u_lo = sb("u_hi", [P, DT, TOK], F32R), sb("u_lo", [P, DT, TOK], F32R)
    scratch = place[0]
    h_hi, h_lo = sb("h_hi", [P, FT, TOK], F32R), sb("h_lo", [P, FT, TOK], F32R)
    scratch_end = place[0]
    w_raw = sb("w_raw", [P, RAW, 8 * P])
    w_hi, w_lo = sb("w_hi", [P, RING, 8 * P], F32R), sb("w_lo", [P, RING, 8 * P], F32R)
    rstd = sb("rstd", [P, TOK])
    rows_at = place[0]
    tmp = sb("tmp", [P, 2, TOK])
    sumsq, sq = sb("sumsq", [P, TOK]), sb("sq", [P, TOK])
    gains = sb("gains", [P, 7, DT])
    vecs = sb("vecs", [P, 3, DT])
    pool_bs = sb("pool_bs", [P, DT])
    mean_w = sb("mean_w", [P, P])
    ident = sb("ident", [P, P])
    later = sb("later", [P, P])
    corr = sb("corr", [P, GROUPS, 16])
    eps_col, one_col = sb("eps_col", [P, 1]), sb("one_col", [P, 1])
    gate_b, m_first = sb("gate_b", [4, 2]), sb("m_first", [4, 1])
    cols = sb("cols", [P, 44])
    mend = sb("mend", [P, 6, HEADS])
    w_write = sb("w_write", [P, NB, HEADS])
    carry = sb("carry", [P, 4, HEADS])
    ssum = sb("ssum", [P, NB, HEADS])
    dd, hv = sb("dd", [P, NB, HEADS]), sb("hv", [P, NB, HEADS])
    assert place[0] <= nc.sbuf_usable_end, place[0]

    cursor = [scratch]

    def over(name, shape):
        size = 4
        for s in shape[1:]:
            size *= s
        offset = cursor[0]
        cursor[0] += (size + 31) // 32 * 32
        assert cursor[0] <= scratch_end, name
        return sb(name, shape, at=offset)

    ext = over("ext", [P, DT, EXT])
    win_a, win_p = over("win_a", [P, 2, 2, EXT]), over("win_p", [P, 2, 2, EXT])
    pool_y = over("pool_y", [P, 2, TOK])

    cursor[0] = scratch
    q_t = over("q_t", [P, HEADS, TOK])
    junk = sb("junk", [P, DV], at=cursor[0])
    k_t = over("k_t", [P, HEADS, TOK])
    v_one = over("v_one", [P, NB, HEADS, DV + 1])
    k_w = over("k_w", [P, NB, HEADS, P])
    og = over("og", [P, DT, TOK])
    m_b = over("m_b", [P, HEADS, TOK])
    probs = over("probs", [P, HEADS, TOK])
    c_st = over("c_st", [P, 3, HEADS, DV + 1])
    sel = over("sel", [4, HEADS, P])
    row = [sb(f"row{n}", [4, TOK], at=rows_at + n * TOK * 4) for n in range(4)]
    r_a, r_f, r_e, r_m = row

    ps = nc.alloc_psum_tensor("ps", [P, 8, 512], F32)

    def pair(b):
        return ps[:, b:b + 2, 0:HALF]

    def halves(ap):
        return ap.rearrange("p (h n) -> p h n", h=2)

    def f32(ap):
        return ap.bitcast(F32)

    sem = nc.alloc_semaphore
    raw_landed = [sem(f"raw_landed{s}") for s in range(RAW)]
    hi_split, lo_split, unit_used = sem("hi_split"), sem("lo_split"), sem("unit_used")
    x_landed = [sem(f"x_landed{j}") for j in range(DT)]
    consts_landed, consts_made = sem("consts_landed"), sem("consts_made")
    x_ready = sem("x_ready")
    u_hi_ready, u_ready = sem("u_hi_ready"), sem("u_ready")
    sq_step, sumsq_ready = sem("sq_step"), sem("sumsq_ready")
    norm_psum, norm_root, rstd_ready = sem("norm_psum"), sem("norm_root"), sem("rstd_ready")
    dve_order = sem("dve_order")
    stores = sem("stores")

    class Ffn:
        def __init__(self, name, base, norm, u_base, w_in, w_out):
            self.base, self.norm, self.u_base, self.w_in, self.w_out = base, norm, u_base, w_in, w_out
            self.gate_scaled = sem(name + "_gate_scaled")
            self.silu_done = sem(name + "_silu_done")
            self.mul_done = sem(name + "_mul_done")
            self.psum_read = sem(name + "_psum_read")
            self.h_hi_ready = sem(name + "_h_hi_ready")
            self.h_ready = sem(name + "_h_ready")

    ffn_a = Ffn("a", U_A, 0, 0, a["ffn1_in"][0], a["ffn1_out"][0])
    ffn_b = Ffn("b", U_B, 2, 8, a["ffn2_in"][0], a["ffn2_out"][0])
    ffn_c = Ffn("c", U_C, 3, 16, a["ffn1_in"][1], a["ffn1_out"][1])
    ffn_d = Ffn("d", U_D, 5, 32, a["ffn2_in"][1], a["ffn2_out"][1])
    N_POOL, N_MIX, N_FINAL = 1, 4, 6

    hist_landed, ext_zero, ext_scaled = sem("hist_landed"), sem("ext_zero"), sem("ext_scaled")
    pool_win, pool_win_step = sem("pool_win"), sem("pool_win_step")
    diff_ready, diff_hi, diff_lo = sem("diff_ready"), sem("diff_hi"), sem("diff_lo")
    pool_psum, pool_y_ready = sem("pool_psum"), sem("pool_y_ready")
    pool_out_done, m_out_done, c_out_done = sem("pool_out_done"), sem("m_out_done"), sem("c_out_done")
    state_landed, sel_made = sem("state_landed"), sem("sel_made")
    proj_read = sem("proj_read")
    gate_abs, gate_exp, gate_log = sem("gate_abs"), sem("gate_exp"), sem("gate_log")
    rows_ready, enm_row = sem("rows_ready"), sem("enm_row")
    core_psum, dve_took, act_took = sem("core_psum"), sem("dve_took"), sem("act_took")
    ends_ready, factors_ready = sem("ends_ready"), sem("factors_ready")
    expo_ready, expo_done = sem("expo_ready"), sem("expo_done")
    q_factor, q_scaled = sem("q_factor"), sem("q_scaled")
    upd_psum, state_ready = sem("upd_psum"), sem("state_ready")
    out_psum, out_read = sem("out_psum"), sem("out_read")
    act_order, squares = sem("act_order"), sem("squares")
    var_ready, root_done, scale_ready, h_scaled = (
        sem("var_ready"), sem("root_done"), sem("scale_ready"), sem("h_scaled"))
    og_ready = sem("og_ready")
    y_psum, y_read, y_hi, y_lo = sem("y_psum"), sem("y_read"), sem("y_hi"), sem("y_lo")
    out_tile = sem("out_tile")

    def block_cols(c):
        return c * CH, (CH if c < NB - 1 else DEC_SEQ)

    AFTER_V = [[("cols", 0), ("mb", 0)], [("mb", 1), ("mb", 2)], [("mb", 3), ("vt", 0)],
               [("vt", 1), ("sk", 0)], [("vt", 2), ("sk", 1)], [("vt", 3), ("sk", 2)],
               [("vt", 4), ("vt", 5), ("sk", 3)], [("vt", 6), ("sk", 4)], [("vt", 7)]]
    ITEM_AT = [sum(map(len, AFTER_V[:t])) for t in range(10)]
    ALL_ITEMS = sum(AFTER_V, [])

    def taken(k):
        on_dve = [kind in ("cols", "sk") for kind, _ in ALL_ITEMS[:k + 1]]
        return (dve_took, sum(on_dve)) if on_dve[k] else (act_took, k + 1 - sum(on_dve))

    IN_O = [(("vt", 7), ("upd", 0)), (("out", 0), ("upd", 1)), (("out", 1), ("upd", 2)),
            (("out", 2), ("upd", 3)), (("out", 3), ("upd", 4)), (("out", 4), None),
            (None, None), (None, None)]
    ROUNDS = [(0, 2, CH), (2, 4, CH), (4, 5, DEC_SEQ)]
    BEFORE_ROOT = [2, 4, 5]
    Y_BANK = [4, 6, 0, 2, 4, 6, 4, 6]
    Y_FREE = [0, 0, 0, 0, 1, 2, 5, 6]

    def old_state(c):
        return (1, 0) if c == NB - 1 else (2 * ((c + 1) % 2), 2 * (c % 2))

    block = nc.Block()
    with block as block:

        @block.sync
        def _(sp):
            def load(n, src, i=0, step=0):
                if n >= RAW:
                    sp.wait_ge(lo_split, n - RAW + 1 + step * i)
                sp.dma_start(w_raw[:, n % RAW, 0:src.shape[1]], src).then_inc(raw_landed[n % RAW], 16)

            def load_ffn(f, first=0):
                for n in range(first):
                    load(f.base + n, f.w_in[n, :, :])
                with sp.Fori(first // 2, FT) as i:
                    for s in range(2):
                        sp.wait_ge(lo_split, f.base + s - RAW + 1 + 2 * i)
                        slot = (f.base + s) % RAW
                        sp.dma_start(w_raw[:, slot, :], f.w_in[2 * i + s, :, :]) \
                            .then_inc(raw_landed[slot], 16)
                with sp.Fori(0, DT // 2) as i:
                    for jj in range(2):
                        k = 0
                        for s, size in enumerate(OUT_UNIT):
                            n = f.base + U_IN + 3 * jj + s
                            sp.wait_ge(lo_split, n - RAW + 1 + 6 * i)
                            sp.dma_start(w_raw[:, n % RAW, 0:size * P],
                                         f.w_out[2 * i + jj, :, k * P:(k + size) * P]) \
                                .then_inc(raw_landed[n % RAW], 16)
                            k += size

            load_ffn(ffn_a, first=2)
            for g in range(GROUPS):
                load(U_POOL + g, a["pool_w"][g, :, :])
            load_ffn(ffn_b)
            load_ffn(ffn_c)
            load(U_M, a["mlstm_gates"])
            with sp.Fori(0, N_PROJ // 2) as i:
                for s in range(2):
                    n = U_M + 1 + s
                    sp.wait_ge(lo_split, n - RAW + 1 + 2 * i)
                    sp.dma_start(w_raw[:, n % RAW, :], a["mlstm_in"][2 * i + s, :, :]) \
                        .then_inc(raw_landed[n % RAW], 16)
            with sp.Fori(0, DT // 2) as i:
                for s in range(2):
                    n = U_MOUT + s
                    sp.wait_ge(lo_split, n - RAW + 1 + 2 * i)
                    sp.dma_start(w_raw[:, n % RAW, :], a["mlstm_out"][2 * i + s, :, :]) \
                        .then_inc(raw_landed[n % RAW], 16)
            load_ffn(ffn_d)
            for j in range(DT):
                sp.wait_ge(out_tile, j + 1)
                sp.dma_start(a["y_prompt"][:, j, :], x[:, j, 0:SEQ]).then_inc(stores, 16)
                sp.dma_start(a["y_sample"][:, j, :], x[:, j, SEQ:TOK]).then_inc(stores, 16)
            sp.wait_ge(stores, 16 * 2 * DT)

        @block.gpsimd
        def _(pool):
            pool.memset(mean_w[:, :], 1.0 / D_MODEL)
            pool.memset(eps_col[:, :], EPS)
            pool.memset(one_col[:, :], 1.0)
            pool.memset(ident[:, :], 0.0)
            pool.memset(later[:, :], 0.0)
            for g in range(GROUPS):
                w = 2 << g
                for t in range(w - 1):
                    pool.memset(corr[:, g, t:t + 1], w / (t + 1.0))
            pool.memset(dd[:, :, :], 0.0).then_inc(consts_made, 1)
            pool.wait_ge(consts_made, 1)
            pool.affine_select(out=ident[:, :], in_=ident[:, :], compare_op=ALU.not_equal, fill=1.0,
                               base=0, pattern=[[-1, P]], channel_multiplier=1)
            pool.affine_select(out=later[:, :], in_=later[:, :], compare_op=ALU.is_ge, fill=1e30,
                               base=0, pattern=[[1, P]], channel_multiplier=-1).then_inc(consts_made, 1)

            steps = [0]

            def square(j):
                if j == 0:
                    pool.tensor_tensor(sumsq[:, :], x[:, j, :], x[:, j, :], ALU.mult).then_inc(sq_step, 1)
                    steps[0] += 1
                    return
                pool.wait_ge(sq_step, steps[0])
                pool.tensor_tensor(sq[:, :], x[:, j, :], x[:, j, :], ALU.mult).then_inc(sq_step, 1)
                steps[0] += 1
                pool.wait_ge(sq_step, steps[0])
                add = pool.tensor_tensor(sumsq[:, :], sumsq[:, :], sq[:, :], ALU.add)
                if j < DT - 1:
                    add.then_inc(sq_step, 1)
                    steps[0] += 1
                else:
                    add.then_inc(sumsq_ready, 1)

            def squares_after(norm):
                pool.wait_ge(norm_psum, norm)
                for j in range(DT):
                    pool.wait_ge(x_ready, DT * norm + j + 1)
                    square(j)

            for j in range(DT):
                pool.wait_ge(x_landed[j], 32)
                square(j)
            squares_after(1)

            g = GROUPS - 1
            pool.wait_ge(norm_psum, 2)
            pool.memset(ext[:, :, 0:HIST], 0.0).then_inc(ext_zero, 1)
            pool.dma_start(ext[:, :, PROMPT0 + SEQ:SAMPLE0], a["pool_hist"]).then_inc(hist_landed, 16)
            pool.wait_ge(ext_scaled, 1)
            pool.wait_ge(rstd_ready, N_POOL + 1)
            for j in (2 * g, 2 * g + 1):
                pool.tensor_tensor(ext[:, j, PROMPT0:PROMPT0 + SEQ], ext[:, j, PROMPT0:PROMPT0 + SEQ],
                                   rstd[:, 0:SEQ], ALU.mult).then_inc(pool_win_step, 1)
                pool.tensor_tensor(ext[:, j, SAMPLE0:EXT], ext[:, j, SAMPLE0:EXT],
                                   rstd[:, SEQ:TOK], ALU.mult).then_inc(pool_win_step, 1)
            pool.wait_ge(ext_zero, 1)
            pool.wait_ge(hist_landed, 16)
            pool.wait_ge(pool_win_step, 4)
            src, width = ext[:, 2 * g:2 * g + 2, :], 1
            for s in range(g + 1):
                dst = win_p[:, s % 2, :, :]
                lo = 2 * width - 1
                add = pool.tensor_tensor(dst[:, :, lo:EXT], src[:, :, lo:EXT],
                                         src[:, :, lo - width:EXT - width], ALU.add)
                if s < g:
                    add.then_inc(pool_win_step, 1)
                    pool.wait_ge(pool_win_step, 5 + s)
                else:
                    add.then_inc(pool_win, 1)
                src, width = dst, 2 * width
            squares_after(2)
            squares_after(3)
            squares_after(4)

            pool.wait_ge(norm_psum, N_MIX + 1)
            pool.memset(sel[:, :, :], 0.0).then_inc(sel_made, 1)
            pool.wait_ge(sel_made, 1)
            pool.affine_select(out=sel[:, :, :], in_=sel[:, :, :], compare_op=ALU.not_equal, fill=1.0,
                               base=0, pattern=[[-1, HEADS], [0, P]], channel_multiplier=1) \
                .then_inc(sel_made, 1)
            pool.memset(v_one[:, :, :, DV:DV + 1], 1.0).then_inc(sel_made, 1)
            for c in range(NB):
                _, n = block_cols(c)
                pool.wait_ge(scale_ready, c // 2 + 1)
                pool.tensor_tensor(v_one[0:n, c, :, 0:DV], v_one[0:n, c, :, 0:DV],
                                   dd[0:n, c, :].unsqueeze(2).to_broadcast([n, HEADS, DV]), ALU.mult) \
                    .then_inc(h_scaled, 1)
            squares_after(5)
            squares_after(6)

        @block.scalar
        def _(act):
            for j in range(DT):
                act.dma_start(x[:, j, 0:SEQ], a["x_prompt"][:, j, :]).then_inc(x_landed[j], 16)
                act.dma_start(x[:, j, SEQ:TOK], a["x_sample"][:, j, :]).then_inc(x_landed[j], 16)
                if j == 0:
                    act.dma_start(gains[:, :, :], a["gains"]).then_inc(consts_landed, 16)
            act.dma_start(vecs[:, :, :], a["vecs"]).then_inc(consts_landed, 16)
            act.dma_start(gate_b[:, :], a["gate_b"]).then_inc(consts_landed, 16)
            act.dma_start(m_first[:, :], a["state_m"]).then_inc(consts_landed, 16)

            def hi(n, i=0):
                size = unit_blocks(n) * P
                if n >= U_END:
                    return
                act.wait_ge(raw_landed[n % RAW], 16 * (n // RAW + 1) + 32 * i)
                if n >= RING:
                    act.wait_ge(unit_used, n - RING + 1 + RING * i)
                if n == U_M:
                    src = w_raw[:, n % RAW, 0:64].rearrange("p (k g c) -> p k g c", k=8, g=2)
                    dst = w_hi[:, n % RING, :].rearrange("p (k g c) -> p k g c", k=8, g=4)
                    act.activation(dst[:, :, 0:2, 0:4], src, ACT.Copy).then_inc(hi_split, 1)
                else:
                    act.activation(w_hi[:, n % RING, 0:size], w_raw[:, n % RAW, 0:size], ACT.Copy) \
                        .then_inc(hi_split, 1)

            def u_high(j, norm):
                act.activation(u_hi[:, j, :], x[:, j, :], ACT.Copy, scale=gains[:, norm, j:j + 1]) \
                    .then_inc(u_hi_ready, 1)

            def root(norm):
                act.wait_ge(norm_psum, norm + 1)
                act.activation(halves(rstd[:, :]), pair(6), ACT.Sqrt, bias=eps_col[:, :]) \
                    .then_inc(norm_root, 1)

            def ffn(f, next_norm):
                root(f.norm)

                def tile(n, t, i):
                    hi(n, i)
                    act.wait_ge(f.gate_scaled, 2 * i + t + 1)
                    act.activation(tmp[:, t, :], tmp[:, t, :], ACT.Silu).then_inc(f.silu_done, 1)
                    hi(n + 1, i)
                    act.wait_ge(f.psum_read, 2 * i + t + 1)
                    act.activation(h_hi[:, 2 * i + t, :], tmp[:, t, :], ACT.Copy) \
                        .then_inc(f.h_hi_ready, 1)

                with act.Fori(0, FT // 2 - 1) as i:
                    for t in range(2):
                        tile(f.base + RING + 2 * t, t, i)
                for t in range(2):
                    act_i = FT // 2 - 1
                    n = f.base + RING + 2 * t + RING * act_i
                    hi(n)
                    act.wait_ge(f.gate_scaled, 2 * act_i + t + 1)
                    act.activation(tmp[:, t, :], tmp[:, t, :], ACT.Silu).then_inc(f.silu_done, 1)
                    hi(n + 1)
                    act.wait_ge(f.psum_read, 2 * act_i + t + 1)
                    act.activation(h_hi[:, 2 * act_i + t, :], tmp[:, t, :], ACT.Copy) \
                        .then_inc(f.h_hi_ready, 1)
                for j in range(DT):
                    n = f.base + U_IN + 3 * j + RING
                    hi(n)
                    hi(n + 1)
                    if next_norm is not None:
                        act.wait_ge(x_ready, DT * (f.norm + 1) + j + 1)
                        u_high(j, next_norm)
                    hi(n + 2)

            hi(0)
            act.wait_ge(consts_landed, 64)
            for j in range(DT):
                act.wait_ge(x_landed[j], 32)
                u_high(j, 0)
                if j % 2 == 1 and j < 7:
                    hi((j + 1) // 2)
            act.wait_ge(consts_made, 2)
            ffn(ffn_a, None)

            root(N_POOL)
            act.wait_ge(x_ready, 2 * DT)
            for j in (DT - 2, DT - 1):
                act.activation(ext[:, j, PROMPT0:PROMPT0 + SEQ], x[:, j, 0:SEQ], ACT.Copy,
                               scale=gains[:, N_POOL, j:j + 1])
                last = act.activation(ext[:, j, SAMPLE0:EXT], x[:, j, SEQ:TOK], ACT.Copy,
                                      scale=gains[:, N_POOL, j:j + 1])
            last.then_inc(ext_scaled, 1)

            def pool_out(g):
                for m in range(2):
                    j = 2 * g + m
                    if m == 0:
                        act.wait_ge(pool_psum, g + 1)
                    else:
                        act.wait_ge(unit_used, U_POOL + g + 1)
                    if j >= 2:
                        act.wait_ge(x_ready, 2 * DT + j - 1)
                    act.activation(halves(pool_y[:, m, :]), pair(2 * (j % 2)), ACT.Identity,
                                   scale=vecs[:, 1, j:j + 1], bias=pool_bs[:, j:j + 1]) \
                        .then_inc(pool_y_ready, 1)
                for m in range(2):
                    act.wait_ge(x_ready, 2 * DT + 2 * g + m + 1)
                    u_high(2 * g + m, 2)
                hi(U_B + g)

            for g in range(GROUPS):
                act.wait_ge(diff_ready, g + 1)
                act.activation(u_hi[:, 2 * g:2 * g + 2, :], tmp[:, :, :], ACT.Copy).then_inc(diff_hi, 1)
                if g >= 1:
                    pool_out(g - 1)
            act.dma_start(a["pool_prompt"], ext[:, :, PROMPT0 + SEQ - HIST:PROMPT0 + SEQ]) \
                .then_inc(pool_out_done, 16)
            act.dma_start(a["pool_sample"], ext[:, :, EXT - HIST:EXT]).then_inc(pool_out_done, 16)
            pool_out(GROUPS - 1)
            act.wait_ge(pool_out_done, 32)
            ffn(ffn_b, 3)
            ffn(ffn_c, 4)

            root(N_MIX)
            act.dma_start(c_st[:, 1, :, :], a["state_c"]).then_inc(state_landed, 16)
            hi(U_M + RING)
            for g in range(1, 9):
                if g == 1:
                    act.wait_ge(gate_abs, 1)
                    act.activation(r_e[:, :], r_e[:, :], ACT.Exp, scale=-1.0).then_inc(gate_exp, 1)
                    act.wait_ge(gate_exp, 1)
                    act.activation(r_e[:, :], r_e[:, :], ACT.Ln, bias=one_col[0:4, :]).then_inc(gate_log, 1)
                if g == 5:
                    act.wait_ge(rows_ready, 1)
                    act.activation(r_e[:, :], r_f[:, :], ACT.Exp, scale=-1.0).then_inc(enm_row, 1)
                    act.dma_start(a["m_prompt"], r_f[:, SEQ - 1:SEQ]).then_inc(m_out_done, 16)
                    act.dma_start(a["m_sample"], r_f[:, TOK - 1:TOK]).then_inc(m_out_done, 16)
                hi(U_M + RING + g)

            def item(kind, n, k):
                b = 4 + 2 * (k % 2)
                if kind == "mb":
                    act.wait_ge(core_psum, k + 1)
                    act.activation(halves(m_b[:, n, :]), pair(b), ACT.Copy).then_inc(act_took, 1)
                elif kind == "vt":
                    act.wait_ge(core_psum, k + 1)
                    h, d0 = n // 2, n % 2 * P
                    act.activation(v_one[:, 0:NB - 1, h, d0:d0 + P],
                                   ps[:, b, :].rearrange("p (c d) -> p c d", c=NB - 1), ACT.Copy)
                    act.activation(v_one[0:DEC_SEQ, NB - 1, h, d0:d0 + P], ps[0:DEC_SEQ, b + 1, 0:P],
                                   ACT.Copy).then_inc(act_took, 1)
                elif kind == "sk":
                    c0, L = block_cols(n)
                    if n == 0:
                        act.wait_ge(ends_ready, 1)
                        act.activation(w_write[:, 0:NB - 1, :], w_write[:, 0:NB - 1, :], ACT.Exp)
                        act.activation(w_write[0:DEC_SEQ, NB - 1, :], w_write[0:DEC_SEQ, NB - 1, :], ACT.Exp)
                        act.activation(carry[:, :, :], carry[:, :, :], ACT.Exp).then_inc(factors_ready, 1)
                    act.wait_ge(expo_ready, n + 1)
                    act.activation(probs[0:L, :, c0:c0 + L], probs[0:L, :, c0:c0 + L], ACT.Exp, scale=-1.0) \
                        .then_inc(expo_done, 1)
                    if n >= 1:
                        before = n - 1 if n < NB - 1 else 4
                        for h in range(HEADS):
                            last = act.activation(m_b[:, h, c0:c0 + L], m_b[:, h, c0:c0 + L], ACT.Exp,
                                                  scale=-1.0, bias=mend[:, before, h:h + 1])
                        last.then_inc(q_factor, 1)

            for t in range(DT):
                hi(U_M + RING + 9 + t)
                for k, (kind, n) in enumerate(AFTER_V[t], ITEM_AT[t]):
                    item(kind, n, k)
            order = 0
            for j in range(DT):
                middle, _ = IN_O[j]
                if middle and middle[0] == "vt":
                    item("vt", 7, ITEM_AT[8])
                elif middle:
                    c = middle[1]
                    _, L = block_cols(c)
                    act.wait_ge(out_read, c + 1)
                    for h in range(HEADS):
                        last = act.activation(junk[0:L, :], v_one[0:L, c, h, 0:DV], ACT.Square,
                                              accum_out=ssum[0:L, c, h:h + 1])
                        if h < HEADS - 1:
                            last.then_inc(act_order, 1)
                            order += 1
                            act.wait_ge(act_order, order)
                    last.then_inc(squares, 1)
                if j - 1 in BEFORE_ROOT:
                    r = BEFORE_ROOT.index(j - 1)
                    first, end, L = ROUNDS[r]
                    act.wait_ge(var_ready, r + 1)
                    act.activation(hv[0:L, first:end, :], hv[0:L, first:end, :], ACT.Sqrt,
                                   scale=1.0 / DV, bias=eps_col[0:L, :]).then_inc(root_done, 1)
                hi(U_M + RING + 17 + j)
                act.wait_ge(proj_read, 18 + j + 1)
                act.activation(og[:, j, :], og[:, j, :], ACT.Sigmoid).then_inc(og_ready, 1)
            act.wait_ge(state_ready, NB)
            act.dma_start(a["c_prompt"], c_st[:, 2, :, :]).then_inc(c_out_done, 16)
            act.dma_start(a["c_sample"], c_st[:, 0, :, :]).then_inc(c_out_done, 16)
            for j in range(DT):
                act.wait_ge(y_read, j + 1)
                act.activation(u_hi[:, j, :], tmp[:, j % 2, :], ACT.Copy).then_inc(y_hi, 1)
            for j in range(DT):
                hi(U_MOUT + RING + j)
            act.wait_ge(unit_used, U_D)
            for j in range(DT):
                act.wait_ge(x_ready, 5 * DT + j + 1)
                u_high(j, 5)
            act.wait_ge(c_out_done, 32)
            ffn(ffn_d, None)
            root(N_FINAL)

        @block.vector
        def _(dve):
            order = [0]

            def link(ins):
                order[0] += 1
                ins.then_inc(dve_order, 1)
                dve.wait_ge(dve_order, order[0])

            def lo(n, i=0):
                size = unit_blocks(n) * P
                if n >= U_END:
                    return
                dve.wait_ge(hi_split, n + 1 + RING * i)
                if n == U_M:
                    src = w_raw[:, n % RAW, 0:64].rearrange("p (k g c) -> p k g c", k=8, g=2)
                    parts = [w[:, n % RING, :].rearrange("p (k g c) -> p k g c", k=8, g=4)[:, :, 0:2, 0:4]
                             for w in (w_hi, w_lo)]
                    dve.tensor_tensor(parts[1], src, f32(parts[0]), ALU.subtract).then_inc(lo_split, 1)
                else:
                    dve.tensor_tensor(w_lo[:, n % RING, 0:size], w_raw[:, n % RAW, 0:size],
                                      f32(w_hi[:, n % RING, 0:size]), ALU.subtract).then_inc(lo_split, 1)

            def u_low(j, norm, count):
                dve.wait_ge(u_hi_ready, count)
                dve.scalar_tensor_tensor(u_lo[:, j, :], x[:, j, :], gains[:, norm, j:j + 1],
                                         f32(u_hi[:, j, :]), ALU.mult, ALU.subtract).then_inc(u_ready, 1)

            def rstd_of(norm):
                dve.wait_ge(norm_root, norm + 1)
                dve.reciprocal(rstd[:, :], rstd[:, :]).then_inc(rstd_ready, 1)
                dve.wait_ge(rstd_ready, norm + 1)

            def scaled(dst, bank):
                return dve.tensor_tensor(halves(dst), pair(bank), halves(rstd[:, :]), ALU.mult)

            def ffn(f, next_norm, next_u):
                rstd_of(f.norm)

                def tile(t, i, ahead):
                    used = f.base + 2 * t + RING * i
                    dve.wait_ge(unit_used, used + 1)
                    scaled(tmp[:, t, :], 4 * t).then_inc(f.gate_scaled, 1)
                    ahead(0)
                    dve.wait_ge(f.silu_done, 2 * i + t + 1)
                    dve.tensor_tensor(tmp[:, t, :], tmp[:, t, :], rstd[:, :], ALU.mult) \
                        .then_inc(f.mul_done, 1)
                    dve.wait_ge(f.mul_done, 2 * i + t + 1)
                    dve.wait_ge(unit_used, used + 2)
                    dve.tensor_tensor(halves(tmp[:, t, :]), halves(tmp[:, t, :]), pair(4 * t + 2), ALU.mult) \
                        .then_inc(f.psum_read, 1)
                    ahead(1)
                    dve.wait_ge(f.h_hi_ready, 2 * i + t + 1)
                    dve.tensor_tensor(h_lo[:, 2 * i + t, :], tmp[:, t, :], f32(h_hi[:, 2 * i + t, :]),
                                      ALU.subtract).then_inc(f.h_ready, 1)

                with dve.Fori(0, FT // 2 - 1) as i:
                    for t in range(2):
                        tile(t, i, lambda s: lo(f.base + RING + 2 * t + s, i))
                last = FT // 2 - 1
                for t in range(2):
                    tile(t, last, lambda s: lo(f.base + RING + 2 * t + s + RING * last))
                for j in range(DT):
                    n = f.base + U_IN + 3 * j + RING
                    lo(n)
                    lo(n + 1)
                    dve.wait_ge(unit_used, f.base + U_IN + 3 * j + 3)
                    dve.scalar_tensor_tensor(halves(x[:, j, :]), pair(2 * (j % 2)), 0.5,
                                             halves(x[:, j, :]), ALU.mult, ALU.add).then_inc(x_ready, 1)
                    if next_norm is not None:
                        u_low(j, next_norm, next_u + j + 1)
                    lo(n + 2)

            lo(0)
            dve.wait_ge(consts_landed, 64)
            for j in range(DT):
                dve.wait_ge(x_landed[j], 32)
                u_low(j, 0, j + 1)
                if j % 2 == 1 and j < 7:
                    lo((j + 1) // 2)
            dve.tensor_tensor(pool_bs[:, :], vecs[:, 0, :], vecs[:, 1, :], ALU.mult) \
                .then_inc(x_ready, DT)
            ffn(ffn_a, None, 0)

            rstd_of(N_POOL)
            dve.wait_ge(consts_made, 2)

            def pool_x(g):
                for m in range(2):
                    j = 2 * g + m
                    dve.wait_ge(pool_y_ready, j + 1)
                    dve.tensor_tensor(x[:, j, :], x[:, j, :], pool_y[:, m, :], ALU.add).then_inc(x_ready, 1)
                for m in range(2):
                    u_low(2 * g + m, 2, DT + 2 * g + m + 1)
                lo(U_B + g)

            for g in range(GROUPS):
                w = 2 << g
                if g < GROUPS - 1:
                    for j in (2 * g, 2 * g + 1):
                        dve.scalar_tensor_tensor(ext[:, j, PROMPT0:PROMPT0 + SEQ], x[:, j, 0:SEQ],
                                                 gains[:, N_POOL, j:j + 1], rstd[:, 0:SEQ], ALU.mult, ALU.mult)
                        last = dve.scalar_tensor_tensor(ext[:, j, SAMPLE0:EXT], x[:, j, SEQ:TOK],
                                                        gains[:, N_POOL, j:j + 1], rstd[:, SEQ:TOK],
                                                        ALU.mult, ALU.mult)
                    link(last)
                    if g == 0:
                        dve.wait_ge(ext_zero, 1)
                        dve.wait_ge(hist_landed, 16)
                    src, width = ext[:, 2 * g:2 * g + 2, :], 1
                    for s in range(g + 1):
                        dst = win_a[:, s % 2, :, :]
                        first = 2 * width - 1
                        link(dve.tensor_tensor(dst[:, :, first:EXT], src[:, :, first:EXT],
                                               src[:, :, first - width:EXT - width], ALU.add))
                        src, width = dst, 2 * width
                else:
                    dve.wait_ge(pool_win, 1)
                    src = win_p[:, g % 2, :, :]
                head = src[:, :, PROMPT0:PROMPT0 + w - 1]
                link(dve.tensor_tensor(head, head,
                                       corr[:, g, 0:w - 1].unsqueeze(1).to_broadcast([P, 2, w - 1]), ALU.mult))
                for t0, e0, n in ((0, PROMPT0, SEQ), (SEQ, SAMPLE0, DEC_SEQ)):
                    last = dve.scalar_tensor_tensor(tmp[:, :, t0:t0 + n], src[:, :, e0:e0 + n], 1.0 / w,
                                                    ext[:, 2 * g:2 * g + 2, e0:e0 + n], ALU.mult, ALU.subtract)
                last.then_inc(diff_ready, 1)
                dve.wait_ge(diff_hi, g + 1)
                dve.tensor_tensor(u_lo[:, 2 * g:2 * g + 2, :], tmp[:, :, :], f32(u_hi[:, 2 * g:2 * g + 2, :]),
                                  ALU.subtract).then_inc(diff_lo, 1)
                if g >= 1:
                    pool_x(g - 1)
            pool_x(GROUPS - 1)
            ffn(ffn_b, 3, 16)
            ffn(ffn_c, 4, 24)

            rstd_of(N_MIX)
            dve.wait_ge(unit_used, U_M + 1)
            dve.tensor_tensor(halves(r_f[:, :]), ps[32:36, 0:2, 0:HALF], halves(rstd[32:36, :]), ALU.mult) \
                .then_inc(proj_read, 1)
            last = dve.tensor_tensor(halves(r_a[:, :]), ps[0:4, 0:2, 0:HALF], halves(rstd[0:4, :]), ALU.mult)
            last.then_inc(proj_read, 1)
            dve.wait_ge(proj_read, 2)
            link(dve.tensor_scalar(r_f[:, :], r_f[:, :], gate_b[:, 1:2], None, ALU.add))
            dve.tensor_scalar(r_a[:, :], r_a[:, :], gate_b[:, 0:1], None, ALU.add)
            dve.scalar_tensor_tensor(r_e[:, :], r_f[:, :], -1.0, r_f[:, :], ALU.mult, ALU.max) \
                .then_inc(gate_abs, 1)
            lo(U_M + RING)
            for g in range(1, 9):
                dve.wait_ge(unit_used, U_M + g + 1)
                b = 2 * (g % 2)
                if g <= 4:
                    dve.scalar_tensor_tensor(halves(q_t[:, g - 1, :]), pair(b), float(P) ** -0.5,
                                             halves(rstd[:, :]), ALU.mult, ALU.mult).then_inc(proj_read, 1)
                else:
                    scaled(k_t[:, g - 5, :], b).then_inc(proj_read, 1)
                if g == 2:
                    dve.wait_ge(gate_log, 1)
                    link(dve.scalar_tensor_tensor(r_f[:, :], r_f[:, :], 0.0, r_e[:, :], ALU.min, ALU.subtract))
                    dve.tensor_tensor_scan(r_e[:, 0:SEQ], r_f[:, 0:SEQ], r_f[:, 0:SEQ], 0.0, ALU.add, ALU.min)
                    link(dve.tensor_tensor_scan(r_e[:, SEQ:TOK], r_f[:, SEQ:TOK], r_f[:, SEQ:TOK], 0.0,
                                                ALU.add, ALU.min))
                if g == 3:
                    link(dve.tensor_tensor(r_a[:, :], r_a[:, :], r_e[:, :], ALU.subtract))
                    dve.tensor_tensor_scan(r_m[:, 0:SEQ], r_a[:, 0:SEQ], r_a[:, 0:SEQ], 0.0, ALU.max, ALU.max)
                    link(dve.tensor_tensor_scan(r_m[:, SEQ:TOK], r_a[:, SEQ:TOK], r_a[:, SEQ:TOK],
                                                m_first[:, :], ALU.max, ALU.max))
                    dve.tensor_tensor(r_f[:, :], r_e[:, :], r_m[:, :], ALU.add).then_inc(rows_ready, 1)
                lo(U_M + RING + g)

            def item(kind, n, k):
                b = 4 + 2 * (k % 2)
                if kind == "cols":
                    dve.wait_ge(core_psum, k + 1)
                    dve.tensor_copy(cols[:, 0:36], ps[:, b, 0:36])
                    dve.tensor_copy(cols[0:DEC_SEQ, 36:44], ps[0:DEC_SEQ, b, 36:44]).then_inc(dve_took, 1)
                elif kind == "mb" and n == HEADS - 1:
                    dve.wait_ge(*taken(k))
                    dve.tensor_copy(mend[:, 0:4, :], m_b[:, :, CH - 1:SEQ:CH].transpose([0, 2, 1]))
                    dve.tensor_copy(mend[:, 4, :], cols[:, 32:36])
                    link(dve.tensor_copy(mend[:, 5, :], m_b[:, :, TOK - 1]))
                    dve.tensor_tensor(w_write[:, 0:4, :], cols[:, 0:16].rearrange("p (c h) -> p c h", c=4),
                                      mend[:, 0:4, :], ALU.subtract)
                    dve.tensor_tensor(w_write[0:DEC_SEQ, 4, :], cols[0:DEC_SEQ, 36:40], mend[0:DEC_SEQ, 5, :],
                                      ALU.subtract)
                    dve.tensor_tensor(carry[:, 0:3, :], mend[:, 0:3, :], mend[:, 1:4, :], ALU.subtract)
                    dve.tensor_tensor(carry[:, 3, :], mend[:, 4, :], mend[:, 5, :], ALU.subtract) \
                        .then_inc(ends_ready, 1)
                elif kind == "sk":
                    c0, L = block_cols(n)
                    a0 = 4 * n if n < NB - 1 else 36
                    for h in range(HEADS):
                        last = dve.scalar_tensor_tensor(probs[0:L, h, c0:c0 + L], m_b[0:L, h, c0:c0 + L],
                                                        cols[0:L, a0 + h:a0 + h + 1], later[0:L, 0:L],
                                                        ALU.subtract, ALU.max)
                    last.then_inc(expo_ready, 1)
                    dve.wait_ge(factors_ready, 1)
                    dve.wait_ge(core_psum, k + 1)
                    dve.tensor_tensor(k_w[0:L, n, :, :], ps[0:L, b + 1, :].rearrange("p (h d) -> p h d", h=4),
                                      w_write[0:L, n, :].unsqueeze(2).to_broadcast([L, HEADS, P]), ALU.mult)
                    dve.wait_ge(expo_done, n + 1)
                    dve.tensor_tensor(probs[0:L, :, c0:c0 + L], probs[0:L, :, c0:c0 + L],
                                      ps[0:L, b, 0:HEADS * L].rearrange("p (h t) -> p h t", h=HEADS),
                                      ALU.mult).then_inc(dve_took, 1)
                    if n >= 1:
                        dve.wait_ge(q_factor, n)
                        dve.tensor_tensor(q_t[:, :, c0:c0 + L], q_t[:, :, c0:c0 + L], m_b[:, :, c0:c0 + L],
                                          ALU.mult).then_inc(q_scaled, 1)

            for t in range(DT):
                dve.wait_ge(unit_used, U_M + 9 + t + 1)
                scaled(og[:, t, :], 2 * ((9 + t) % 2)).then_inc(proj_read, 1)
                lo(U_M + RING + 9 + t)
                for k, (kind, n) in enumerate(AFTER_V[t], ITEM_AT[t]):
                    item(kind, n, k)

            def chunk(kind, c):
                _, L = block_cols(c)
                old, new = old_state(c)
                if kind == "upd":
                    dve.wait_ge(upd_psum, c + 1)
                    if c == 0:
                        dve.tensor_copy(c_st[:, new, :, :], ps[:, 4:8, 0:DV + 1]).then_inc(state_ready, 1)
                        return
                    if c == NB - 1:
                        dve.wait_ge(state_landed, 16)
                    else:
                        dve.wait_ge(state_ready, c)
                    for h in range(HEADS):
                        last = dve.scalar_tensor_tensor(
                            c_st[:, new, h, :], c_st[:, old, h, :],
                            carry[:, c - 1:c, h], ps[:, 4 + h, 0:DV + 1], ALU.mult, ALU.add)
                    last.then_inc(state_ready, 1)
                elif kind == "out":
                    dve.wait_ge(out_psum, c + 1)
                    dve.tensor_copy(v_one[0:L, c, :, :], ps[0:L, 4:8, 0:DV + 1]).then_inc(out_read, 1)

            def variance(r):
                first, end, L = ROUNDS[r]
                den = v_one[0:L, first:end, :, DV]
                d, v = dd[0:L, first:end, :], hv[0:L, first:end, :]
                e0 = 16 + 4 * first if first < NB - 1 else 40
                enm = cols[0:L, e0:e0 + 4 * (end - first)].rearrange("p (c h) -> p c h", h=HEADS)
                dve.wait_ge(squares, end)
                link(dve.scalar_tensor_tensor(d, den, -1.0, den, ALU.mult, ALU.max))
                link(dve.tensor_tensor(d, d, enm, ALU.max))
                link(dve.reciprocal(d, d))
                link(dve.tensor_tensor(v, d, d, ALU.mult))
                dve.tensor_tensor(v, v, ssum[0:L, first:end, :], ALU.mult).then_inc(var_ready, 1)

            def head_scale(r):
                first, end, L = ROUNDS[r]
                d, v = dd[0:L, first:end, :], hv[0:L, first:end, :]
                dve.wait_ge(root_done, r + 1)
                link(dve.reciprocal(v, v))
                dve.tensor_tensor(d, d, v, ALU.mult).then_inc(scale_ready, 1)

            for j in range(DT):
                middle, behind = IN_O[j]
                if middle and middle[0] == "out":
                    chunk(*middle)
                dve.wait_ge(unit_used, U_M + 17 + j + 1)
                scaled(og[:, j, :], 2 * ((17 + j) % 2)).then_inc(proj_read, 1)
                lo(U_M + RING + 17 + j)
                if behind:
                    chunk(*behind)
                if j in BEFORE_ROOT:
                    variance(BEFORE_ROOT.index(j))
                if j - 1 in BEFORE_ROOT:
                    head_scale(BEFORE_ROOT.index(j - 1))

            def y_low(j):
                dve.wait_ge(y_hi, j + 1)
                dve.tensor_tensor(u_lo[:, j, :], tmp[:, j % 2, :], f32(u_hi[:, j, :]), ALU.subtract) \
                    .then_inc(y_lo, 1)

            dve.wait_ge(m_out_done, 32)
            for j in range(DT):
                b = Y_BANK[j]
                dve.wait_ge(y_psum, j + 1)
                dve.wait_ge(og_ready, j + 1)
                if j >= 2:
                    dve.wait_ge(y_lo, j - 1)
                dve.scalar_tensor_tensor(tmp[:, j % 2, 0:SEQ], ps[:, b, :], vecs[:, 2, j:j + 1],
                                         og[:, j, 0:SEQ], ALU.mult, ALU.mult)
                dve.scalar_tensor_tensor(tmp[:, j % 2, SEQ:TOK], ps[:, b + 1, 0:DEC_SEQ], vecs[:, 2, j:j + 1],
                                         og[:, j, SEQ:TOK], ALU.mult, ALU.mult).then_inc(y_read, 1)
                if j >= 1:
                    y_low(j - 1)
            y_low(DT - 1)
            for j in range(DT):
                dve.wait_ge(unit_used, U_MOUT + j + 1)
                dve.tensor_tensor(halves(x[:, j, :]), halves(x[:, j, :]), pair(2 * (j % 2)), ALU.add) \
                    .then_inc(x_ready, 1)
                lo(U_MOUT + RING + j)
            for j in range(DT):
                u_low(j, 5, 4 * DT + j + 1)
            ffn(ffn_d, None, 0)

            rstd_of(N_FINAL)
            for j in range(DT):
                dve.scalar_tensor_tensor(x[:, j, :], x[:, j, :], gains[:, N_FINAL, j:j + 1], rstd[:, :],
                                         ALU.mult, ALU.mult).then_inc(out_tile, 1)

        @block.tensor
        def _(pe):
            def block_mm(n, kk, k, bank, first, last):
                w_h, w_l = (w[:, n % RING, kk * P:(kk + 1) * P] for w in (w_hi, w_lo))
                m_h, m_l = k
                for p, (w, m) in enumerate(((w_h, m_h), (w_h, m_l), (w_l, m_h))):
                    for h in range(2):
                        mm = pe.matmul(ps[:, bank + h, 0:HALF], w, m[:, h * HALF:(h + 1) * HALF],
                                       start=first and p == 0, stop=last and p == 2)
                return mm

            def u_tile(k):
                return u_hi[:, k, :], u_lo[:, k, :]

            def project(n, bank, i=0, ready=None, base=0, middle=None):
                pe.wait_ge(lo_split, n + 1 + RING * i)
                for k in range(DT):
                    if ready is not None:
                        pe.wait_ge(ready, base + k + 1)
                    mm = block_mm(n, k, u_tile(k), bank, k == 0, k == DT - 1)
                    if k == DT - 1:
                        mm.then_inc(unit_used, 1)
                    if k == 3 and middle:
                        middle()

            def norm(n):
                pe.wait_ge(sumsq_ready, n + 1)
                for h in range(2):
                    mm = pe.matmul(ps[:, 6 + h, 0:HALF], mean_w[:, :], sumsq[:, h * HALF:(h + 1) * HALF],
                                   start=True, stop=True)
                mm.then_inc(norm_psum, 1)

            def ffn(f):
                for t in range(2):
                    if t == 0 and f.norm:
                        pe.wait_ge(x_ready, DT * (f.norm + 1) - 1)
                    project(f.base + 2 * t, 4 * t, ready=u_ready if t == 0 else None, base=f.u_base)
                    if t == 0:
                        norm(f.norm)
                        if f.norm:
                            pe.wait_ge(x_ready, DT * (f.norm + 1))
                    else:
                        pe.wait_ge(norm_root, f.norm + 1)
                    project(f.base + 2 * t + 1, 4 * t + 2)
                with pe.Fori(1, FT // 2) as i:
                    for t in range(2):
                        pe.wait_ge(f.psum_read, 2 * i + t - 1)
                        project(f.base + 2 * t, 4 * t, i)
                        project(f.base + 2 * t + 1, 4 * t + 2, i)
                with pe.Fori(0, DT // 4) as i:
                    for jj in range(4):
                        pe.wait_ge(f.psum_read, FT - 1)
                        pe.wait_ge(x_ready, DT * (f.norm + 1) + (4 * i + jj - 1 if jj else 3 * i))
                        k = 0
                        for s, size in enumerate(OUT_UNIT):
                            n = f.base + U_IN + 3 * jj + s
                            pe.wait_ge(lo_split, n + 1 + 3 * 4 * i)
                            for kk in range(size):
                                if jj == 0:
                                    pe.wait_ge(f.h_ready, k + 1)
                                mm = block_mm(n, kk, (h_hi[:, k, :], h_lo[:, k, :]), 2 * (jj % 2),
                                              k == 0, k == FT - 1)
                                k += 1
                            mm.then_inc(unit_used, 1)

            pe.wait_ge(consts_made, 2)
            ffn(ffn_a)

            pe.wait_ge(x_ready, 2 * DT)
            norm(N_POOL)
            for g in range(GROUPS):
                pe.wait_ge(lo_split, U_POOL + g + 1)
                pe.wait_ge(diff_lo, g + 1)
                for m in range(2):
                    j = 2 * g + m
                    if j >= 2:
                        pe.wait_ge(pool_y_ready, j - 1)
                    for k in range(2):
                        mm = block_mm(U_POOL + g, 2 * k + m, u_tile(2 * g + k), 2 * (j % 2), k == 0, k == 1)
                    mm.then_inc((pool_psum, unit_used)[m], 1)
            ffn(ffn_b)
            ffn(ffn_c)

            pe.wait_ge(x_ready, 5 * DT - 1)
            project(U_M, 0, ready=u_ready, base=3 * DT)
            norm(N_MIX)
            pe.wait_ge(x_ready, 5 * DT)
            with pe.Fori(0, 2) as i:
                for c in range(4):
                    pe.wait_ge(proj_read, 4 * i + c + 1)
                    project(U_M + 1 + c, 2 * ((1 + c) % 2), i)

            def item(kind, n, k):
                b = 4 + 2 * (k % 2)
                if k >= 2:
                    pe.wait_ge(*taken(k - 2))
                if k == 1:
                    pe.wait_ge(norm_root, N_MIX + 1)
                if kind == "cols":
                    pe.wait_ge(enm_row, 1)
                    pe.wait_ge(sel_made, 3)
                    for c in range(NB):
                        c0, L = block_cols(c)
                        for r, rows in enumerate((r_a, r_e)):
                            o = 16 * r + 4 * c if c < NB - 1 else 36 + 4 * r
                            pe.matmul(ps[0:L, b, o:o + 4], rows[:, c0:c0 + L], ident[0:4, 0:4],
                                      start=True, stop=True)
                    for h in range(HEADS):
                        mm = pe.matmul(ps[:, b, 32 + h:33 + h], sel[:, h, :], m_first[:, :],
                                       start=True, stop=True)
                elif kind == "mb":
                    for h in range(2):
                        mm = pe.matmul(ps[:, b + h, 0:HALF], sel[:, n, :], r_m[:, h * HALF:(h + 1) * HALF],
                                       start=True, stop=True)
                elif kind == "vt":
                    pe.wait_ge(proj_read, 10 + n + 1)
                    for c in range(NB - 1):
                        pe.transpose(ps[:, b, c * CH:(c + 1) * CH], og[:, n, c * CH:(c + 1) * CH], ident[:, :])
                    mm = pe.matmul(ps[0:DEC_SEQ, b + 1, 0:P], og[:, n, SEQ:TOK], ident[:, :],
                                   start=True, stop=True)
                elif kind == "sk":
                    c0, L = block_cols(n)
                    for h in range(HEADS):
                        k_c = k_t[:, h, c0:c0 + L]
                        pe.matmul(ps[0:L, b, h * L:(h + 1) * L], k_c, q_t[:, h, c0:c0 + L],
                                  start=True, stop=True)
                        if L == P:
                            mm = pe.transpose(ps[:, b + 1, h * P:(h + 1) * P], k_c, ident[:, :])
                        else:
                            mm = pe.matmul(ps[0:L, b + 1, h * P:(h + 1) * P], k_c, ident[:, :],
                                           start=True, stop=True)
                mm.then_inc(core_psum, 1)

            def chunk(kind, c):
                c0, L = block_cols(c)
                old, _ = old_state(c)
                if kind == "upd":
                    if c == 0:
                        pe.wait_ge(*taken(ITEM_AT[9] - 2))
                        pe.wait_ge(*taken(ITEM_AT[9] - 1))
                    else:
                        pe.wait_ge(out_read, c)
                    for h in range(HEADS):
                        mm = pe.matmul(ps[:, 4 + h, 0:DV + 1], k_w[0:L, c, h, :], v_one[0:L, c, h, :],
                                       start=True, stop=True)
                    mm.then_inc(upd_psum, 1)
                else:
                    pe.wait_ge(state_ready, c + 1)
                    if c:
                        pe.wait_ge(q_scaled, c)
                    if c == NB - 1:
                        pe.wait_ge(state_landed, 16)
                    for h in range(HEADS):
                        mm = pe.matmul(ps[0:L, 4 + h, 0:DV + 1], probs[0:L, h, c0:c0 + L],
                                       v_one[0:L, c, h, :], start=True, stop=c == 0)
                        if c:
                            mm = pe.matmul(ps[0:L, 4 + h, 0:DV + 1], q_t[:, h, c0:c0 + L],
                                           c_st[:, old, h, :], start=False, stop=True)
                    mm.then_inc(out_psum, 1)

            for t in range(DT):
                pe.wait_ge(proj_read, 9 + t)
                project(U_M + 9 + t, 2 * ((9 + t) % 2))
                for k, (kind, n) in enumerate(AFTER_V[t], ITEM_AT[t]):
                    item(kind, n, k)

            def in_o(what):
                if what and what[0] == "vt":
                    item("vt", 7, ITEM_AT[8])
                elif what:
                    chunk(*what)

            for j in range(DT):
                pe.wait_ge(proj_read, 17 + j)
                middle, behind = IN_O[j]
                project(U_M + 17 + j, 2 * ((17 + j) % 2), middle=lambda: in_o(middle))
                in_o(behind)
            pe.wait_ge(h_scaled, NB)
            for j in range(DT):
                b = Y_BANK[j]
                h, d0 = j // 2, j % 2 * P
                if j == 2:
                    pe.wait_ge(proj_read, 26)
                if j >= 4:
                    pe.wait_ge(y_read, Y_FREE[j])
                for c in range(NB - 1):
                    pe.transpose(ps[:, b, c * CH:(c + 1) * CH], v_one[:, c, h, d0:d0 + P], ident[:, :])
                pe.matmul(ps[:, b + 1, 0:DEC_SEQ], v_one[0:DEC_SEQ, NB - 1, h, d0:d0 + P],
                          ident[0:DEC_SEQ, 0:DEC_SEQ], start=True, stop=True).then_inc(y_psum, 1)
            pe.wait_ge(y_read, 4)
            with pe.Fori(0, DT // 4) as i:
                for c in range(4):
                    pe.wait_ge(x_ready, 5 * DT + 4 * i + c - 1)
                    project(U_MOUT + c, 2 * (c % 2), i, ready=y_lo if c == 0 else None)
            ffn(ffn_d)
            pe.wait_ge(x_ready, 7 * DT)
            norm(N_FINAL)


def _tiles(v):
    return v.reshape((DT, P) + v.shape[1:]).swapaxes(0, 1)


def kernel(x_prompt, x_sample, state_pool, state_mlstm_C, state_mlstm_n, state_mlstm_m, norm_ffn1,
           ffn1_w_in, ffn1_w_out, norm_mix, pool_w, pool_b, pool_scale, mlstm_w_in, mlstm_b_i, mlstm_b_f,
           mlstm_norm, mlstm_w_out, norm_ffn2, ffn2_w_in, ffn2_w_out, norm_final):
    import numpy as np
    import concourse.bacc as bacc
    from concourse.bass_utils import run_bass_kernel_spmd

    def ffn_in(w):
        return np.asarray(w).reshape(2, DT, P, 2, FT, P).transpose(0, 4, 3, 2, 1, 5).reshape(2, 2 * FT, P, DT * P)

    def ffn_out(w):
        return np.asarray(w).reshape(2, FT, P, DT, P).transpose(0, 3, 2, 1, 4).reshape(2, DT, P, FT * P)

    def square_w(w, n):
        return np.asarray(w).reshape(DT, P, n, P).transpose(2, 1, 0, 3).reshape(n, P, DT * P)

    w_mix = np.asarray(mlstm_w_in)[0]
    f1, mx, f2 = np.asarray(norm_ffn1), np.asarray(norm_mix), np.asarray(norm_ffn2)
    gains = np.stack([f1[0], mx[0], f2[0], f1[1], mx[1], f2[1], np.asarray(norm_final)], 1)
    vecs = np.stack([np.asarray(v)[0] for v in (pool_b, pool_scale, mlstm_norm)], 1)
    ins = {
        "x_prompt": _tiles(np.asarray(x_prompt)[0].T),
        "x_sample": _tiles(np.asarray(x_sample)[0].T),
        "pool_hist": _tiles(np.asarray(state_pool)[0, 0].T),
        "state_c": np.concatenate([np.asarray(state_mlstm_C)[0, 0].transpose(2, 0, 1),
                                   np.asarray(state_mlstm_n)[0, 0].T[:, :, None]], 2),
        "state_m": np.asarray(state_mlstm_m)[0, 0].reshape(HEADS, 1),
        "gains": _tiles(gains).transpose(0, 2, 1),
        "vecs": _tiles(vecs).transpose(0, 2, 1),
        "gate_b": np.stack([np.asarray(mlstm_b_i)[0], np.asarray(mlstm_b_f)[0]], 1),
        "ffn1_in": ffn_in(ffn1_w_in), "ffn1_out": ffn_out(ffn1_w_out),
        "ffn2_in": ffn_in(ffn2_w_in), "ffn2_out": ffn_out(ffn2_w_out),
        "pool_w": np.asarray(pool_w)[0].reshape(GROUPS, 2, P, 2 * P).transpose(0, 2, 1, 3).reshape(GROUPS, P, 4 * P),
        "mlstm_in": square_w(w_mix[:, :N_PROJ * P], N_PROJ),
        "mlstm_gates": _tiles(w_mix[:, N_PROJ * P:]).reshape(P, DT * 2 * HEADS),
        "mlstm_out": square_w(np.asarray(mlstm_w_out)[0], DT),
    }
    outs = {
        "y_prompt": (P, DT, SEQ), "y_sample": (P, DT, DEC_SEQ),
        "pool_prompt": (P, DT, HIST), "pool_sample": (P, DT, HIST),
        "c_prompt": (P, HEADS, DV + 1), "c_sample": (P, HEADS, DV + 1),
        "m_prompt": (HEADS, 1), "m_sample": (HEADS, 1),
    }
    nc = bacc.Bacc("TRN2", target_bir_lowering=False, num_devices=1)
    arrays, aps = {}, {}
    for name, v in ins.items():
        arrays["in_" + name] = np.ascontiguousarray(v)
        aps[name] = nc.dram_tensor("in_" + name, v.shape, mybir.dt.from_np(v.dtype), kind="ExternalInput").ap()
    for name, shape in outs.items():
        aps[name] = nc.dram_tensor("out_" + name, shape, mybir.dt.float32, kind="ExternalOutput").ap()
    encoder_step(nc, aps)
    got = run_bass_kernel_spmd(nc, [arrays], core_ids=[0]).results[0]
    r = {name: got["out_" + name] for name in outs}

    def rows(v):
        return np.ascontiguousarray(v.transpose(2, 1, 0).reshape(1, v.shape[2], D_MODEL))

    def state(v):
        return (np.ascontiguousarray(v[:, :, :DV].transpose(1, 2, 0))[None, None],
                np.ascontiguousarray(v[:, :, DV].T)[None, None])

    c_p, n_p = state(r["c_prompt"])
    c_s, n_s = state(r["c_sample"])
    return (rows(r["y_prompt"]), rows(r["y_sample"]), rows(r["pool_prompt"])[None], c_p, n_p,
            r["m_prompt"].reshape(1, 1, HEADS), rows(r["pool_sample"])[None], c_s, n_s,
            r["m_sample"].reshape(1, 1, HEADS))
```

```python
import concourse.bass as bass
from concourse import mybir

P = 128
D_MODEL = 1024
DT = D_MODEL // P
SEQ, DEC_SEQ = 512, 64
TOK = SEQ + DEC_SEQ
HALF = TOK // 2
D_FF = 2816
FT = D_FF // P
HIST = 15
GROUPS = 4
EXT = TOK + 2 * HIST
PROMPT0, SAMPLE0 = HIST, HIST + SEQ + HIST
HEADS = 4
DV = 256
CH = 128
NB = SEQ // CH + 1
EPS = 1e-6
RING, RAW = 4, 2

U_IN, U_OUT = 2 * FT, 3 * DT
FFN_UNITS = U_IN + U_OUT
U_A = 0
U_POOL = U_A + FFN_UNITS
U_B = U_POOL + GROUPS
U_C = U_B + FFN_UNITS
U_M = U_C + FFN_UNITS
N_PROJ = 3 * DT
U_MOUT = U_M + 1 + N_PROJ
U_D = U_MOUT + DT
U_END = U_D + FFN_UNITS
OUT_UNIT = (8, 8, 6)


def unit_blocks(n):
    for start in (U_A, U_B, U_C, U_D):
        if start + U_IN <= n < start + FFN_UNITS:
            return OUT_UNIT[(n - start - U_IN) % 3]
    if U_POOL <= n < U_B:
        return 4
    return 8


def encoder_step(nc, a):
    F32, F32R = mybir.dt.float32, mybir.dt.float32r
    ALU, ACT = mybir.AluOpType, mybir.ActivationFunctionType

    place = [(nc.sbuf_base + 63) // 64 * 64]

    def sb(name, shape, dt=F32, at=None):
        size = 4
        for s in shape[1:]:
            size *= s
        offset = place[0] if at is None else at
        if at is None:
            place[0] += (size + 31) // 32 * 32
        return nc.alloc_sbuf_tensor_at(name, shape, dt, offset=offset)

    x = sb("x", [P, DT, TOK])
    u_hi, u_lo = sb("u_hi", [P, DT, TOK], F32R), sb("u_lo", [P, DT, TOK], F32R)
    scratch = place[0]
    h_hi, h_lo = sb("h_hi", [P, FT, TOK], F32R), sb("h_lo", [P, FT, TOK], F32R)
    scratch_end = place[0]
    w_raw = sb("w_raw", [P, RAW, 8 * P])
    w_hi, w_lo = sb("w_hi", [P, RING, 8 * P], F32R), sb("w_lo", [P, RING, 8 * P], F32R)
    rstd = sb("rstd", [P, TOK])
    rows_at = place[0]
    tmp = sb("tmp", [P, 2, TOK])
    sumsq, sq = sb("sumsq", [P, TOK]), sb("sq", [P, TOK])
    gains = sb("gains", [P, 7, DT])
    vecs = sb("vecs", [P, 3, DT])
    pool_bs = sb("pool_bs", [P, DT])
    mean_w = sb("mean_w", [P, P])
    warm = sb("warm", [P, 1])
    rms_col = sb("rms_col", [P, 40])
    ident = sb("ident", [P, P])
    later = sb("later", [P, P])
    corr = sb("corr", [P, GROUPS, 16])
    eps_col, one_col = sb("eps_col", [P, 1]), sb("one_col", [P, 1])
    gate_b, m_first = sb("gate_b", [4, 2]), sb("m_first", [4, 1])
    cols = sb("cols", [P, 44])
    mend = sb("mend", [P, 6, HEADS])
    w_write = sb("w_write", [P, NB, HEADS])
    carry = sb("carry", [P, 4, HEADS])
    ssum = sb("ssum", [P, NB, HEADS])
    dd, hv = sb("dd", [P, NB, HEADS]), sb("hv", [P, NB, HEADS])
    assert place[0] <= nc.sbuf_usable_end, place[0]

    cursor = [scratch]

    def over(name, shape):
        size = 4
        for s in shape[1:]:
            size *= s
        offset = cursor[0]
        cursor[0] += (size + 31) // 32 * 32
        assert cursor[0] <= scratch_end, name
        return sb(name, shape, at=offset)

    ext = over("ext", [P, DT, EXT])
    win_a, win_p = over("win_a", [P, 2, 2, EXT]), over("win_p", [P, 2, 2, EXT])
    pool_y = over("pool_y", [P, 2, TOK])

    cursor[0] = scratch
    q_t = over("q_t", [P, HEADS, TOK])
    junk = sb("junk", [P, DV], at=cursor[0])
    k_t = over("k_t", [P, HEADS, TOK])
    v_one = over("v_one", [P, NB, HEADS, DV + 1])
    k_w = over("k_w", [P, NB, HEADS, P])
    og = over("og", [P, DT, TOK])
    m_b = over("m_b", [P, HEADS, TOK])
    probs = over("probs", [P, HEADS, TOK])
    c_st = over("c_st", [P, 3, HEADS, DV + 1])
    sel = over("sel", [4, HEADS, P])
    cursor[0] = scratch
    diag = over("diag", [P, NB, P])
    row = [sb(f"row{n}", [4, TOK], at=rows_at + n * TOK * 4) for n in range(4)]
    r_a, r_f, r_e, r_m = row

    ps = nc.alloc_psum_tensor("ps", [P, 8, 512], F32)

    def pair(b):
        return ps[:, b:b + 2, 0:HALF]

    def halves(ap):
        return ap.rearrange("p (h n) -> p h n", h=2)

    def f32(ap):
        return ap.bitcast(F32)

    sem = nc.alloc_semaphore
    raw_landed = [sem(f"raw_landed{s}") for s in range(RAW)]
    hi_split, lo_split, unit_used = sem("hi_split"), sem("lo_split"), sem("unit_used")
    x_landed = [sem(f"x_landed{j}") for j in range(DT)]
    gains_landed, consts_landed = sem("gains_landed"), sem("consts_landed")
    mean_made, consts_made = sem("mean_made"), sem("consts_made")
    x_ready = sem("x_ready")
    u_hi_ready, u_ready = sem("u_hi_ready"), sem("u_ready")
    sq_step, sumsq_ready = sem("sq_step"), sem("sumsq_ready")
    sq_last = sem("sq_last")
    norm_psum, norm_root, rstd_ready = sem("norm_psum"), sem("norm_root"), sem("rstd_ready")
    diag_ready, spread, rstd_copied = sem("diag_ready"), sem("spread"), sem("rstd_copied")
    dve_order = sem("dve_order")
    stores = sem("stores")

    class Ffn:
        def __init__(self, name, base, norm, u_base, w_in, w_out):
            self.base, self.norm, self.u_base, self.w_in, self.w_out = base, norm, u_base, w_in, w_out
            self.gate_scaled = sem(name + "_gate_scaled")
            self.silu_done = sem(name + "_silu_done")
            self.mul_done = sem(name + "_mul_done")
            self.psum_read = sem(name + "_psum_read")
            self.h_hi_ready = sem(name + "_h_hi_ready")
            self.h_ready = sem(name + "_h_ready")

    ffn_a = Ffn("a", U_A, 0, 0, a["ffn1_in"][0], a["ffn1_out"][0])
    ffn_b = Ffn("b", U_B, 2, 8, a["ffn2_in"][0], a["ffn2_out"][0])
    ffn_c = Ffn("c", U_C, 3, 16, a["ffn1_in"][1], a["ffn1_out"][1])
    ffn_d = Ffn("d", U_D, 5, 32, a["ffn2_in"][1], a["ffn2_out"][1])
    N_POOL, N_MIX, N_FINAL = 1, 4, 6
    N_POOL_OUT = 2

    hist_landed, ext_zero, ext_scaled = sem("hist_landed"), sem("ext_zero"), sem("ext_scaled")
    pool_win, pool_win_step = sem("pool_win"), sem("pool_win_step")
    diff_ready, diff_hi, diff_lo = sem("diff_ready"), sem("diff_hi"), sem("diff_lo")
    pool_psum, pool_y_ready = sem("pool_psum"), sem("pool_y_ready")
    pool_out_done, m_out_done, c_out_done = sem("pool_out_done"), sem("m_out_done"), sem("c_out_done")
    state_landed, sel_made = sem("state_landed"), sem("sel_made")
    proj_read = sem("proj_read")
    gate_abs, gate_exp, gate_log = sem("gate_abs"), sem("gate_exp"), sem("gate_log")
    rows_ready, enm_row = sem("rows_ready"), sem("enm_row")
    core_psum, dve_took, act_took = sem("core_psum"), sem("dve_took"), sem("act_took")
    ends_ready, factors_ready = sem("ends_ready"), sem("factors_ready")
    expo_ready, expo_done = sem("expo_ready"), sem("expo_done")
    q_factor, q_scaled = sem("q_factor"), sem("q_scaled")
    upd_psum, state_ready = sem("upd_psum"), sem("state_ready")
    out_psum, out_read = sem("out_psum"), sem("out_read")
    act_order, squares = sem("act_order"), sem("squares")
    var_ready, root_done, scale_ready, h_scaled = (
        sem("var_ready"), sem("root_done"), sem("scale_ready"), sem("h_scaled"))
    og_ready, u_free = sem("og_ready"), sem("u_free")
    y_psum, y_read, y_hi, y_lo = sem("y_psum"), sem("y_read"), sem("y_hi"), sem("y_lo")
    out_tile, out_pool = sem("out_tile"), sem("out_pool")

    SAMPLE_COL = 39

    def block_cols(c):
        return c * CH, (CH if c < NB - 1 else DEC_SEQ)

    FIRST_UNITS = [0, 4, 6]
    AFTER_V = [[("cols", 0), ("mb", 0)], [("mb", 1), ("mb", 2)], [("mb", 3), ("vt", 0)],
               [("vt", 1), ("sk", 0)], [("vt", 2), ("sk", 1)], [("vt", 3), ("sk", 2)],
               [("vt", 4), ("vt", 5), ("sk", 3)], [("vt", 6), ("sk", 4)], [("vt", 7)]]
    ITEM_AT = [sum(map(len, AFTER_V[:t])) for t in range(10)]
    ALL_ITEMS = sum(AFTER_V, [])

    def taken(k):
        on_dve = [kind in ("cols", "sk") for kind, _ in ALL_ITEMS[:k + 1]]
        return (dve_took, sum(on_dve)) if on_dve[k] else (act_took, k + 1 - sum(on_dve))

    IN_O = [(("vt", 7), ("upd", 0)), (("out", 0), ("upd", 1)), (("out", 1), ("upd", 2)),
            (("out", 2), ("upd", 3)), (("out", 3), ("upd", 4)), (("out", 4), None),
            (None, None), (None, None)]
    ROUNDS = [(0, 2, CH), (2, 4, CH), (4, 5, DEC_SEQ)]
    BEFORE_ROOT = [2, 4, 5]

    def old_state(c):
        return (1, 0) if c == NB - 1 else (2 * ((c + 1) % 2), 2 * (c % 2))

    block = nc.Block()
    with block as block:

        @block.sync
        def _(sp):
            def load(n, src, i=0, step=0):
                if n >= RAW:
                    sp.wait_ge(lo_split, n - RAW + 1 + step * i)
                sp.dma_start(w_raw[:, n % RAW, 0:src.shape[1]], src).then_inc(raw_landed[n % RAW], 16)

            def load_ffn(f, first=0):
                for n in range(first):
                    load(f.base + n, f.w_in[n, :, :])
                with sp.Fori(first // 2, FT) as i:
                    for s in range(2):
                        sp.wait_ge(lo_split, f.base + s - RAW + 1 + 2 * i)
                        slot = (f.base + s) % RAW
                        sp.dma_start(w_raw[:, slot, :], f.w_in[2 * i + s, :, :]) \
                            .then_inc(raw_landed[slot], 16)
                with sp.Fori(0, DT // 2) as i:
                    for jj in range(2):
                        k = 0
                        for s, size in enumerate(OUT_UNIT):
                            n = f.base + U_IN + 3 * jj + s
                            sp.wait_ge(lo_split, n - RAW + 1 + 6 * i)
                            sp.dma_start(w_raw[:, n % RAW, 0:size * P],
                                         f.w_out[2 * i + jj, :, k * P:(k + size) * P]) \
                                .then_inc(raw_landed[n % RAW], 16)
                            k += size

            load_ffn(ffn_a, first=2)
            for g in range(GROUPS):
                load(U_POOL + g, a["pool_w"][g, :, :])
            load_ffn(ffn_b)
            load_ffn(ffn_c)
            load(U_M, a["mlstm_gates"])
            with sp.Fori(0, N_PROJ // 2) as i:
                for s in range(2):
                    n = U_M + 1 + s
                    sp.wait_ge(lo_split, n - RAW + 1 + 2 * i)
                    sp.dma_start(w_raw[:, n % RAW, :], a["mlstm_in"][2 * i + s, :, :]) \
                        .then_inc(raw_landed[n % RAW], 16)
            with sp.Fori(0, DT // 2) as i:
                for s in range(2):
                    n = U_MOUT + s
                    sp.wait_ge(lo_split, n - RAW + 1 + 2 * i)
                    sp.dma_start(w_raw[:, n % RAW, :], a["mlstm_out"][2 * i + s, :, :]) \
                        .then_inc(raw_landed[n % RAW], 16)
            load_ffn(ffn_d)
            for j in (2, 3, 0, 4, 5, 1, 6, 7):
                if j < N_POOL_OUT:
                    sp.wait_ge(out_pool, j + 1)
                else:
                    sp.wait_ge(out_tile, j - N_POOL_OUT + 1)
                sp.dma_start(a["y"][:, j, :], x[:, j, :]).then_inc(stores, 16)
            sp.wait_ge(stores, 16 * DT)

        @block.gpsimd
        def _(pool):
            pool.memset(mean_w[:, :], 1.0 / D_MODEL).then_inc(mean_made, 1)
            pool.dma_start(vecs[:, :, :], a["vecs"]).then_inc(consts_landed, 16)
            pool.dma_start(gate_b[:, :], a["gate_b"]).then_inc(consts_landed, 16)
            pool.dma_start(m_first[:, :], a["state_m"]).then_inc(consts_landed, 16)
            pool.memset(eps_col[:, :], EPS)
            pool.memset(one_col[:, :], 1.0)
            pool.memset(ident[:, :], 0.0)
            pool.memset(later[:, :], 0.0)
            for g in range(GROUPS):
                w = 2 << g
                for t in range(w - 1):
                    pool.memset(corr[:, g, t:t + 1], w / (t + 1.0))
            pool.memset(dd[:, :, :], 0.0).then_inc(consts_made, 1)
            pool.wait_ge(consts_made, 1)
            pool.affine_select(out=ident[:, :], in_=ident[:, :], compare_op=ALU.not_equal, fill=1.0,
                               base=0, pattern=[[-1, P]], channel_multiplier=1)
            pool.affine_select(out=later[:, :], in_=later[:, :], compare_op=ALU.is_ge, fill=1e30,
                               base=0, pattern=[[1, P]], channel_multiplier=-1).then_inc(consts_made, 1)

            steps = [0]

            def square(j, last=DT - 1):
                if j == 0:
                    pool.tensor_tensor(sumsq[:, :], x[:, j, :], x[:, j, :], ALU.mult).then_inc(sq_step, 1)
                    steps[0] += 1
                    return
                pool.wait_ge(sq_step, steps[0])
                pool.tensor_tensor(sq[:, :], x[:, j, :], x[:, j, :], ALU.mult).then_inc(sq_step, 1)
                steps[0] += 1
                pool.wait_ge(sq_step, steps[0])
                add = pool.tensor_tensor(sumsq[:, :], sumsq[:, :], sq[:, :], ALU.add)
                if j < last:
                    add.then_inc(sq_step, 1)
                    steps[0] += 1
                else:
                    add.then_inc(sumsq_ready, 1)

            def squares_after(norm, tiles=DT):
                pool.wait_ge(norm_psum, norm)
                for j in range(tiles):
                    pool.wait_ge(x_ready, DT * norm + j + 1)
                    square(j, tiles - 1)

            for j in range(DT):
                pool.wait_ge(x_landed[j], 16)
                square(j)
            squares_after(1)

            g = GROUPS - 1
            pool.wait_ge(norm_psum, 2)
            pool.memset(ext[:, :, 0:HIST], 0.0).then_inc(ext_zero, 1)
            pool.dma_start(ext[:, :, PROMPT0 + SEQ:SAMPLE0], a["pool_hist"]).then_inc(hist_landed, 16)
            pool.wait_ge(ext_scaled, 1)
            pool.wait_ge(rstd_ready, N_POOL + 1)
            for j in (2 * g, 2 * g + 1):
                pool.tensor_tensor(ext[:, j, PROMPT0:PROMPT0 + SEQ], ext[:, j, PROMPT0:PROMPT0 + SEQ],
                                   rstd[:, 0:SEQ], ALU.mult).then_inc(pool_win_step, 1)
                pool.tensor_tensor(ext[:, j, SAMPLE0:EXT], ext[:, j, SAMPLE0:EXT],
                                   rstd[:, SEQ:TOK], ALU.mult).then_inc(pool_win_step, 1)
            pool.wait_ge(ext_zero, 1)
            pool.wait_ge(hist_landed, 16)
            pool.wait_ge(pool_win_step, 4)
            src, width = ext[:, 2 * g:2 * g + 2, :], 1
            for s in range(g + 1):
                dst = win_p[:, s % 2, :, :]
                lo = 2 * width - 1
                add = pool.tensor_tensor(dst[:, :, lo:EXT], src[:, :, lo:EXT],
                                         src[:, :, lo - width:EXT - width], ALU.add)
                if s < g:
                    add.then_inc(pool_win_step, 1)
                    pool.wait_ge(pool_win_step, 5 + s)
                else:
                    add.then_inc(pool_win, 1)
                src, width = dst, 2 * width
            squares_after(2)
            squares_after(3)
            squares_after(4)

            pool.wait_ge(norm_psum, N_MIX + 1)
            pool.memset(sel[:, :, :], 0.0).then_inc(sel_made, 1)
            pool.wait_ge(sel_made, 1)
            pool.affine_select(out=sel[:, :, :], in_=sel[:, :, :], compare_op=ALU.not_equal, fill=1.0,
                               base=0, pattern=[[-1, HEADS], [0, P]], channel_multiplier=1) \
                .then_inc(sel_made, 1)
            pool.memset(v_one[:, :, :, DV:DV + 1], 1.0).then_inc(sel_made, 1)
            for c in range(NB):
                _, n = block_cols(c)
                pool.wait_ge(scale_ready, c // 2 + 1)
                pool.tensor_tensor(v_one[0:n, c, :, 0:DV], v_one[0:n, c, :, 0:DV],
                                   dd[0:n, c, :].unsqueeze(2).to_broadcast([n, HEADS, DV]), ALU.mult) \
                    .then_inc(h_scaled, 1)
            squares_after(5)
            squares_after(6, DT - 1)
            for j in range(N_POOL_OUT):
                pool.wait_ge(rstd_copied, 1)
                pool.tensor_tensor(x[:, j, :], tmp[:, j, :], rstd[:, :], ALU.mult).then_inc(out_pool, 1)

        @block.scalar
        def _(act):
            for j in range(DT):
                act.dma_start(x[:, j, :], a["x"][:, j, :]).then_inc(x_landed[j], 16)
                if j == 0:
                    act.dma_start(gains[:, :, :], a["gains"]).then_inc(gains_landed, 16)
            act.wait_ge(mean_made, 1)
            act.activation(warm[:, :], mean_w[:, 0:1], ACT.Copy)

            def hi(n, i=0):
                size = unit_blocks(n) * P
                if n >= U_END:
                    return
                act.wait_ge(raw_landed[n % RAW], 16 * (n // RAW + 1) + 32 * i)
                if n >= RING:
                    act.wait_ge(unit_used, n - RING + 1 + RING * i)
                if n == U_M:
                    src = w_raw[:, n % RAW, 0:64].rearrange("p (k g c) -> p k g c", k=8, g=2)
                    dst = w_hi[:, n % RING, :].rearrange("p (k g c) -> p k g c", k=8, g=4)
                    act.activation(dst[:, :, 0:2, 0:4], src, ACT.Copy).then_inc(hi_split, 1)
                else:
                    act.activation(w_hi[:, n % RING, 0:size], w_raw[:, n % RAW, 0:size], ACT.Copy) \
                        .then_inc(hi_split, 1)

            def u_high(j, norm):
                act.activation(u_hi[:, j, :], x[:, j, :], ACT.Copy, scale=gains[:, norm, j:j + 1]) \
                    .then_inc(u_hi_ready, 1)

            def root(norm):
                act.wait_ge(norm_psum, norm + 1)
                act.activation(halves(rstd[:, :]), pair(6), ACT.Sqrt, bias=eps_col[:, :]) \
                    .then_inc(norm_root, 1)

            def last_square(norm):
                act.activation(warm[:, :], eps_col[:, :], ACT.Sqrt)
                act.wait_ge(sumsq_ready, norm + 1)
                act.wait_ge(x_ready, DT * (norm + 1))
                act.activation(sq[:, :], x[:, DT - 1, :], ACT.Square).then_inc(sq_last, 1)

            def root_cols(norm, n):
                act.wait_ge(norm_psum, norm + 1)
                act.activation(rms_col[:, 0:n], ps[:, 5, 0:n], ACT.Sqrt, bias=eps_col[:, :])
                act.activation(rms_col[0:DEC_SEQ, SAMPLE_COL:SAMPLE_COL + 1],
                               ps[0:DEC_SEQ, 5, SAMPLE_COL:SAMPLE_COL + 1], ACT.Sqrt,
                               bias=eps_col[0:DEC_SEQ, :]).then_inc(norm_root, 1)

            def ffn(f, next_norm):
                root(f.norm)

                def tile(n, t, i):
                    hi(n, i)
                    act.wait_ge(f.gate_scaled, 2 * i + t + 1)
                    act.activation(tmp[:, t, :], tmp[:, t, :], ACT.Silu).then_inc(f.silu_done, 1)
                    hi(n + 1, i)
                    act.wait_ge(f.psum_read, 2 * i + t + 1)
                    act.activation(h_hi[:, 2 * i + t, :], tmp[:, t, :], ACT.Copy) \
                        .then_inc(f.h_hi_ready, 1)

                with act.Fori(0, FT // 2 - 1) as i:
                    for t in range(2):
                        tile(f.base + RING + 2 * t, t, i)
                for t in range(2):
                    act_i = FT // 2 - 1
                    n = f.base + RING + 2 * t + RING * act_i
                    hi(n)
                    act.wait_ge(f.gate_scaled, 2 * act_i + t + 1)
                    act.activation(tmp[:, t, :], tmp[:, t, :], ACT.Silu).then_inc(f.silu_done, 1)
                    hi(n + 1)
                    act.wait_ge(f.psum_read, 2 * act_i + t + 1)
                    act.activation(h_hi[:, 2 * act_i + t, :], tmp[:, t, :], ACT.Copy) \
                        .then_inc(f.h_hi_ready, 1)
                for j in range(DT):
                    n = f.base + U_IN + 3 * j + RING
                    hi(n)
                    hi(n + 1)
                    if next_norm is not None:
                        act.wait_ge(x_ready, DT * (f.norm + 1) + j + 1)
                        u_high(j, next_norm)
                    hi(n + 2)

            hi(0)
            act.wait_ge(gains_landed, 16)
            for j in range(DT):
                act.wait_ge(x_landed[j], 16)
                u_high(j, 0)
                if j in FIRST_UNITS:
                    hi(FIRST_UNITS.index(j) + 1)
            act.wait_ge(consts_made, 2)
            ffn(ffn_a, None)

            root(N_POOL)
            act.wait_ge(x_ready, 2 * DT)
            for j in (DT - 2, DT - 1):
                act.activation(ext[:, j, PROMPT0:PROMPT0 + SEQ], x[:, j, 0:SEQ], ACT.Copy,
                               scale=gains[:, N_POOL, j:j + 1])
                last = act.activation(ext[:, j, SAMPLE0:EXT], x[:, j, SEQ:TOK], ACT.Copy,
                                      scale=gains[:, N_POOL, j:j + 1])
            last.then_inc(ext_scaled, 1)

            def pool_out(g):
                for m in range(2):
                    j = 2 * g + m
                    if m == 0:
                        act.wait_ge(pool_psum, g + 1)
                    else:
                        act.wait_ge(unit_used, U_POOL + g + 1)
                    if j >= 2:
                        act.wait_ge(x_ready, 2 * DT + j - 1)
                    act.activation(halves(pool_y[:, m, :]), pair(2 * (j % 2)), ACT.Identity,
                                   scale=vecs[:, 1, j:j + 1], bias=pool_bs[:, j:j + 1]) \
                        .then_inc(pool_y_ready, 1)
                for m in range(2):
                    act.wait_ge(x_ready, 2 * DT + 2 * g + m + 1)
                    u_high(2 * g + m, 2)
                hi(U_B + g)

            for g in range(GROUPS):
                act.wait_ge(diff_ready, g + 1)
                act.activation(u_hi[:, 2 * g:2 * g + 2, :], tmp[:, :, :], ACT.Copy).then_inc(diff_hi, 1)
                if g >= 1:
                    pool_out(g - 1)
            act.dma_start(a["pool_prompt"], ext[:, :, PROMPT0 + SEQ - HIST:PROMPT0 + SEQ]) \
                .then_inc(pool_out_done, 16)
            act.dma_start(a["pool_sample"], ext[:, :, EXT - HIST:EXT]).then_inc(pool_out_done, 16)
            pool_out(GROUPS - 1)
            act.wait_ge(pool_out_done, 32)
            ffn(ffn_b, 3)
            ffn(ffn_c, 4)

            root(N_MIX)
            act.dma_start(c_st[:, 1, :, :], a["state_c"]).then_inc(state_landed, 16)
            hi(U_M + RING)
            for g in range(1, 9):
                if g == 1:
                    act.wait_ge(gate_abs, 1)
                    act.activation(r_e[:, :], r_e[:, :], ACT.Exp, scale=-1.0).then_inc(gate_exp, 1)
                    act.wait_ge(gate_exp, 1)
                    act.activation(r_e[:, :], r_e[:, :], ACT.Ln, bias=one_col[0:4, :]).then_inc(gate_log, 1)
                if g == 5:
                    act.wait_ge(rows_ready, 1)
                    act.activation(r_e[:, :], r_f[:, :], ACT.Exp, scale=-1.0).then_inc(enm_row, 1)
                    act.dma_start(a["m_prompt"], r_f[:, SEQ - 1:SEQ]).then_inc(m_out_done, 16)
                    act.dma_start(a["m_sample"], r_f[:, TOK - 1:TOK]).then_inc(m_out_done, 16)
                hi(U_M + RING + g)

            def item(kind, n, k):
                b = 4 + 2 * (k % 2)
                if kind == "mb":
                    act.wait_ge(core_psum, k + 1)
                    act.activation(halves(m_b[:, n, :]), pair(b), ACT.Copy).then_inc(act_took, 1)
                elif kind == "vt":
                    act.wait_ge(core_psum, k + 1)
                    h, d0 = n // 2, n % 2 * P
                    act.activation(v_one[:, 0:NB - 1, h, d0:d0 + P],
                                   ps[:, b, :].rearrange("p (c d) -> p c d", c=NB - 1), ACT.Copy)
                    act.activation(v_one[0:DEC_SEQ, NB - 1, h, d0:d0 + P], ps[0:DEC_SEQ, b + 1, 0:P],
                                   ACT.Copy).then_inc(act_took, 1)
                elif kind == "sk":
                    c0, L = block_cols(n)
                    if n == 0:
                        act.wait_ge(ends_ready, 1)
                        act.activation(w_write[:, 0:NB - 1, :], w_write[:, 0:NB - 1, :], ACT.Exp)
                        act.activation(w_write[0:DEC_SEQ, NB - 1, :], w_write[0:DEC_SEQ, NB - 1, :], ACT.Exp)
                        act.activation(carry[:, :, :], carry[:, :, :], ACT.Exp).then_inc(factors_ready, 1)
                    act.wait_ge(expo_ready, n + 1)
                    act.activation(probs[0:L, :, c0:c0 + L], probs[0:L, :, c0:c0 + L], ACT.Exp, scale=-1.0) \
                        .then_inc(expo_done, 1)
                    if n >= 1:
                        before = n - 1 if n < NB - 1 else 4
                        for h in range(HEADS):
                            last = act.activation(m_b[:, h, c0:c0 + L], m_b[:, h, c0:c0 + L], ACT.Exp,
                                                  scale=-1.0, bias=mend[:, before, h:h + 1])
                        last.then_inc(q_factor, 1)

            for t in range(DT):
                hi(U_M + RING + 9 + t)
                for k, (kind, n) in enumerate(AFTER_V[t], ITEM_AT[t]):
                    item(kind, n, k)
            order = 0
            for j in range(DT):
                middle, _ = IN_O[j]
                if middle and middle[0] == "vt":
                    item("vt", 7, ITEM_AT[8])
                elif middle:
                    c = middle[1]
                    _, L = block_cols(c)
                    act.wait_ge(out_read, c + 1)
                    for h in range(HEADS):
                        last = act.activation(junk[0:L, :], v_one[0:L, c, h, 0:DV], ACT.Square,
                                              accum_out=ssum[0:L, c, h:h + 1])
                        if h < HEADS - 1:
                            last.then_inc(act_order, 1)
                            order += 1
                            act.wait_ge(act_order, order)
                    last.then_inc(squares, 1)
                if j - 1 in BEFORE_ROOT:
                    r = BEFORE_ROOT.index(j - 1)
                    first, end, L = ROUNDS[r]
                    act.wait_ge(var_ready, r + 1)
                    act.activation(hv[0:L, first:end, :], hv[0:L, first:end, :], ACT.Sqrt,
                                   scale=1.0 / DV, bias=eps_col[0:L, :]).then_inc(root_done, 1)
                hi(U_M + RING + 17 + j)
                act.wait_ge(proj_read, 18 + j + 1)
                act.activation(og[:, j, :], og[:, j, :], ACT.Sigmoid).then_inc(og_ready, 1)
            act.wait_ge(state_ready, NB)
            act.dma_start(a["c_prompt"], c_st[:, 2, :, :]).then_inc(c_out_done, 16)
            act.dma_start(a["c_sample"], c_st[:, 0, :, :]).then_inc(c_out_done, 16)
            for j in range(DT):
                act.wait_ge(y_read, j + 1)
                act.activation(u_hi[:, j, :], tmp[:, j % 2, :], ACT.Copy).then_inc(y_hi, 1)
            for j in range(DT - 1):
                hi(U_MOUT + RING + j)
            for j in range(DT):
                if j < DT - 1:
                    act.wait_ge(u_free, j + 1)
                act.wait_ge(x_ready, 5 * DT + j + 1)
                u_high(j, 5)
            hi(U_MOUT + RING + DT - 1)
            act.wait_ge(c_out_done, 32)
            ffn(ffn_d, None)
            for j in range(N_POOL_OUT):
                act.activation(tmp[:, j, :], x[:, j, :], ACT.Copy, scale=gains[:, N_FINAL, j:j + 1])
            last_square(N_FINAL)
            root_cols(N_FINAL, 4)
            act.wait_ge(spread, 1)
            act.activation(halves(rstd[:, :]), pair(6), ACT.Copy).then_inc(rstd_copied, 1)

        @block.vector
        def _(dve):
            order = [0]

            def link(ins):
                order[0] += 1
                ins.then_inc(dve_order, 1)
                dve.wait_ge(dve_order, order[0])

            def lo(n, i=0):
                size = unit_blocks(n) * P
                if n >= U_END:
                    return
                dve.wait_ge(hi_split, n + 1 + RING * i)
                if n == U_M:
                    src = w_raw[:, n % RAW, 0:64].rearrange("p (k g c) -> p k g c", k=8, g=2)
                    parts = [w[:, n % RING, :].rearrange("p (k g c) -> p k g c", k=8, g=4)[:, :, 0:2, 0:4]
                             for w in (w_hi, w_lo)]
                    dve.tensor_tensor(parts[1], src, f32(parts[0]), ALU.subtract).then_inc(lo_split, 1)
                else:
                    dve.tensor_tensor(w_lo[:, n % RING, 0:size], w_raw[:, n % RAW, 0:size],
                                      f32(w_hi[:, n % RING, 0:size]), ALU.subtract).then_inc(lo_split, 1)

            def u_low(j, norm, count):
                dve.wait_ge(u_hi_ready, count)
                dve.scalar_tensor_tensor(u_lo[:, j, :], x[:, j, :], gains[:, norm, j:j + 1],
                                         f32(u_hi[:, j, :]), ALU.mult, ALU.subtract).then_inc(u_ready, 1)

            def rstd_of(norm):
                dve.wait_ge(norm_root, norm + 1)
                dve.reciprocal(rstd[:, :], rstd[:, :]).then_inc(rstd_ready, 1)
                dve.wait_ge(rstd_ready, norm + 1)

            def rstd_cols(norm, n):
                dve.wait_ge(norm_root, norm + 1)
                dve.reciprocal(rms_col[:, 0:n], rms_col[:, 0:n])
                link(dve.reciprocal(rms_col[0:DEC_SEQ, SAMPLE_COL:SAMPLE_COL + 1],
                                    rms_col[0:DEC_SEQ, SAMPLE_COL:SAMPLE_COL + 1]))

            def scaled(dst, bank):
                return dve.tensor_tensor(halves(dst), pair(bank), halves(rstd[:, :]), ALU.mult)

            def ffn(f, next_norm, next_u):
                rstd_of(f.norm)

                def tile(t, i, ahead):
                    used = f.base + 2 * t + RING * i
                    dve.wait_ge(unit_used, used + 1)
                    scaled(tmp[:, t, :], 4 * t).then_inc(f.gate_scaled, 1)
                    ahead(0)
                    dve.wait_ge(f.silu_done, 2 * i + t + 1)
                    dve.tensor_tensor(tmp[:, t, :], tmp[:, t, :], rstd[:, :], ALU.mult) \
                        .then_inc(f.mul_done, 1)
                    dve.wait_ge(f.mul_done, 2 * i + t + 1)
                    dve.wait_ge(unit_used, used + 2)
                    dve.tensor_tensor(halves(tmp[:, t, :]), halves(tmp[:, t, :]), pair(4 * t + 2), ALU.mult) \
                        .then_inc(f.psum_read, 1)
                    ahead(1)
                    dve.wait_ge(f.h_hi_ready, 2 * i + t + 1)
                    dve.tensor_tensor(h_lo[:, 2 * i + t, :], tmp[:, t, :], f32(h_hi[:, 2 * i + t, :]),
                                      ALU.subtract).then_inc(f.h_ready, 1)

                with dve.Fori(0, FT // 2 - 1) as i:
                    for t in range(2):
                        tile(t, i, lambda s: lo(f.base + RING + 2 * t + s, i))
                last = FT // 2 - 1
                for t in range(2):
                    tile(t, last, lambda s: lo(f.base + RING + 2 * t + s + RING * last))
                for j in range(DT):
                    n = f.base + U_IN + 3 * j + RING
                    lo(n)
                    lo(n + 1)
                    dve.wait_ge(unit_used, f.base + U_IN + 3 * j + 3)
                    dve.scalar_tensor_tensor(halves(x[:, j, :]), pair(2 * (j % 2)), 0.5,
                                             halves(x[:, j, :]), ALU.mult, ALU.add).then_inc(x_ready, 1)
                    if next_norm is not None:
                        u_low(j, next_norm, next_u + j + 1)
                    lo(n + 2)

            lo(0)
            dve.wait_ge(gains_landed, 16)
            for j in range(DT):
                dve.wait_ge(x_landed[j], 16)
                u_low(j, 0, j + 1)
                if j in FIRST_UNITS:
                    lo(FIRST_UNITS.index(j) + 1)
            dve.wait_ge(consts_landed, 48)
            dve.tensor_tensor(pool_bs[:, :], vecs[:, 0, :], vecs[:, 1, :], ALU.mult) \
                .then_inc(x_ready, DT)
            ffn(ffn_a, None, 0)

            rstd_of(N_POOL)
            dve.wait_ge(consts_made, 2)

            def pool_x(g):
                for m in range(2):
                    j = 2 * g + m
                    dve.wait_ge(pool_y_ready, j + 1)
                    dve.tensor_tensor(x[:, j, :], x[:, j, :], pool_y[:, m, :], ALU.add).then_inc(x_ready, 1)
                for m in range(2):
                    u_low(2 * g + m, 2, DT + 2 * g + m + 1)
                lo(U_B + g)

            for g in range(GROUPS):
                w = 2 << g
                if g < GROUPS - 1:
                    for j in (2 * g, 2 * g + 1):
                        dve.scalar_tensor_tensor(ext[:, j, PROMPT0:PROMPT0 + SEQ], x[:, j, 0:SEQ],
                                                 gains[:, N_POOL, j:j + 1], rstd[:, 0:SEQ], ALU.mult, ALU.mult)
                        last = dve.scalar_tensor_tensor(ext[:, j, SAMPLE0:EXT], x[:, j, SEQ:TOK],
                                                        gains[:, N_POOL, j:j + 1], rstd[:, SEQ:TOK],
                                                        ALU.mult, ALU.mult)
                    link(last)
                    if g == 0:
                        dve.wait_ge(ext_zero, 1)
                        dve.wait_ge(hist_landed, 16)
                    src, width = ext[:, 2 * g:2 * g + 2, :], 1
                    for s in range(g + 1):
                        dst = win_a[:, s % 2, :, :]
                        first = 2 * width - 1
                        link(dve.tensor_tensor(dst[:, :, first:EXT], src[:, :, first:EXT],
                                               src[:, :, first - width:EXT - width], ALU.add))
                        src, width = dst, 2 * width
                else:
                    dve.wait_ge(pool_win, 1)
                    src = win_p[:, g % 2, :, :]
                head = src[:, :, PROMPT0:PROMPT0 + w - 1]
                link(dve.tensor_tensor(head, head,
                                       corr[:, g, 0:w - 1].unsqueeze(1).to_broadcast([P, 2, w - 1]), ALU.mult))
                for t0, e0, n in ((0, PROMPT0, SEQ), (SEQ, SAMPLE0, DEC_SEQ)):
                    last = dve.scalar_tensor_tensor(tmp[:, :, t0:t0 + n], src[:, :, e0:e0 + n], 1.0 / w,
                                                    ext[:, 2 * g:2 * g + 2, e0:e0 + n], ALU.mult, ALU.subtract)
                last.then_inc(diff_ready, 1)
                dve.wait_ge(diff_hi, g + 1)
                dve.tensor_tensor(u_lo[:, 2 * g:2 * g + 2, :], tmp[:, :, :], f32(u_hi[:, 2 * g:2 * g + 2, :]),
                                  ALU.subtract).then_inc(diff_lo, 1)
                if g >= 1:
                    pool_x(g - 1)
            pool_x(GROUPS - 1)
            ffn(ffn_b, 3, 16)
            ffn(ffn_c, 4, 24)

            rstd_of(N_MIX)
            dve.wait_ge(unit_used, U_M + 1)
            dve.tensor_tensor(halves(r_f[:, :]), ps[32:36, 4:6, 0:HALF], halves(rstd[32:36, :]), ALU.mult) \
                .then_inc(proj_read, 1)
            last = dve.tensor_tensor(halves(r_a[:, :]), ps[0:4, 4:6, 0:HALF], halves(rstd[0:4, :]), ALU.mult)
            last.then_inc(proj_read, 1)
            dve.wait_ge(proj_read, 2)
            link(dve.tensor_scalar(r_f[:, :], r_f[:, :], gate_b[:, 1:2], None, ALU.add))
            dve.tensor_scalar(r_a[:, :], r_a[:, :], gate_b[:, 0:1], None, ALU.add)
            dve.scalar_tensor_tensor(r_e[:, :], r_f[:, :], -1.0, r_f[:, :], ALU.mult, ALU.max) \
                .then_inc(gate_abs, 1)
            lo(U_M + RING)
            for g in range(1, 9):
                dve.wait_ge(unit_used, U_M + g + 1)
                b = 2 * (g % 2)
                if g <= 4:
                    dve.scalar_tensor_tensor(halves(q_t[:, g - 1, :]), pair(b), float(P) ** -0.5,
                                             halves(rstd[:, :]), ALU.mult, ALU.mult).then_inc(proj_read, 1)
                else:
                    scaled(k_t[:, g - 5, :], b).then_inc(proj_read, 1)
                if g == 2:
                    dve.wait_ge(gate_log, 1)
                    link(dve.scalar_tensor_tensor(r_f[:, :], r_f[:, :], 0.0, r_e[:, :], ALU.min, ALU.subtract))
                    dve.tensor_tensor_scan(r_e[:, 0:SEQ], r_f[:, 0:SEQ], r_f[:, 0:SEQ], 0.0, ALU.add, ALU.min)
                    link(dve.tensor_tensor_scan(r_e[:, SEQ:TOK], r_f[:, SEQ:TOK], r_f[:, SEQ:TOK], 0.0,
                                                ALU.add, ALU.min))
                if g == 3:
                    link(dve.tensor_tensor(r_a[:, :], r_a[:, :], r_e[:, :], ALU.subtract))
                    dve.tensor_tensor_scan(r_m[:, 0:SEQ], r_a[:, 0:SEQ], r_a[:, 0:SEQ], 0.0, ALU.max, ALU.max)
                    link(dve.tensor_tensor_scan(r_m[:, SEQ:TOK], r_a[:, SEQ:TOK], r_a[:, SEQ:TOK],
                                                m_first[:, :], ALU.max, ALU.max))
                    dve.tensor_tensor(r_f[:, :], r_e[:, :], r_m[:, :], ALU.add).then_inc(rows_ready, 1)
                lo(U_M + RING + g)

            def item(kind, n, k):
                b = 4 + 2 * (k % 2)
                if kind == "cols":
                    dve.wait_ge(core_psum, k + 1)
                    dve.tensor_copy(cols[:, 0:36], ps[:, b, 0:36])
                    dve.tensor_copy(cols[0:DEC_SEQ, 36:44], ps[0:DEC_SEQ, b, 36:44]).then_inc(dve_took, 1)
                elif kind == "mb" and n == HEADS - 1:
                    dve.wait_ge(*taken(k))
                    dve.tensor_copy(mend[:, 0:4, :], m_b[:, :, CH - 1:SEQ:CH].transpose([0, 2, 1]))
                    dve.tensor_copy(mend[:, 4, :], cols[:, 32:36])
                    link(dve.tensor_copy(mend[:, 5, :], m_b[:, :, TOK - 1]))
                    dve.tensor_tensor(w_write[:, 0:4, :], cols[:, 0:16].rearrange("p (c h) -> p c h", c=4),
                                      mend[:, 0:4, :], ALU.subtract)
                    dve.tensor_tensor(w_write[0:DEC_SEQ, 4, :], cols[0:DEC_SEQ, 36:40], mend[0:DEC_SEQ, 5, :],
                                      ALU.subtract)
                    dve.tensor_tensor(carry[:, 0:3, :], mend[:, 0:3, :], mend[:, 1:4, :], ALU.subtract)
                    dve.tensor_tensor(carry[:, 3, :], mend[:, 4, :], mend[:, 5, :], ALU.subtract) \
                        .then_inc(ends_ready, 1)
                elif kind == "sk":
                    c0, L = block_cols(n)
                    a0 = 4 * n if n < NB - 1 else 36
                    for h in range(HEADS):
                        last = dve.scalar_tensor_tensor(probs[0:L, h, c0:c0 + L], m_b[0:L, h, c0:c0 + L],
                                                        cols[0:L, a0 + h:a0 + h + 1], later[0:L, 0:L],
                                                        ALU.subtract, ALU.max)
                    last.then_inc(expo_ready, 1)
                    dve.wait_ge(factors_ready, 1)
                    dve.wait_ge(core_psum, k + 1)
                    dve.tensor_tensor(k_w[0:L, n, :, :], ps[0:L, b + 1, :].rearrange("p (h d) -> p h d", h=4),
                                      w_write[0:L, n, :].unsqueeze(2).to_broadcast([L, HEADS, P]), ALU.mult)
                    dve.wait_ge(expo_done, n + 1)
                    dve.tensor_tensor(probs[0:L, :, c0:c0 + L], probs[0:L, :, c0:c0 + L],
                                      ps[0:L, b, 0:HEADS * L].rearrange("p (h t) -> p h t", h=HEADS),
                                      ALU.mult).then_inc(dve_took, 1)
                    if n >= 1:
                        dve.wait_ge(q_factor, n)
                        dve.tensor_tensor(q_t[:, :, c0:c0 + L], q_t[:, :, c0:c0 + L], m_b[:, :, c0:c0 + L],
                                          ALU.mult).then_inc(q_scaled, 1)

            for t in range(DT):
                dve.wait_ge(unit_used, U_M + 9 + t + 1)
                scaled(og[:, t, :], 2 * ((9 + t) % 2)).then_inc(proj_read, 1)
                lo(U_M + RING + 9 + t)
                for k, (kind, n) in enumerate(AFTER_V[t], ITEM_AT[t]):
                    item(kind, n, k)

            def chunk(kind, c):
                _, L = block_cols(c)
                old, new = old_state(c)
                if kind == "upd":
                    dve.wait_ge(upd_psum, c + 1)
                    if c == 0:
                        dve.tensor_copy(c_st[:, new, :, :], ps[:, 4:8, 0:DV + 1]).then_inc(state_ready, 1)
                        return
                    if c == NB - 1:
                        dve.wait_ge(state_landed, 16)
                    else:
                        dve.wait_ge(state_ready, c)
                    for h in range(HEADS):
                        last = dve.scalar_tensor_tensor(
                            c_st[:, new, h, :], c_st[:, old, h, :],
                            carry[:, c - 1:c, h], ps[:, 4 + h, 0:DV + 1], ALU.mult, ALU.add)
                    last.then_inc(state_ready, 1)
                elif kind == "out":
                    dve.wait_ge(out_psum, c + 1)
                    dve.tensor_copy(v_one[0:L, c, :, :], ps[0:L, 4:8, 0:DV + 1]).then_inc(out_read, 1)

            def variance(r):
                first, end, L = ROUNDS[r]
                den = v_one[0:L, first:end, :, DV]
                d, v = dd[0:L, first:end, :], hv[0:L, first:end, :]
                e0 = 16 + 4 * first if first < NB - 1 else 40
                enm = cols[0:L, e0:e0 + 4 * (end - first)].rearrange("p (c h) -> p c h", h=HEADS)
                dve.wait_ge(squares, end)
                link(dve.scalar_tensor_tensor(d, den, -1.0, den, ALU.mult, ALU.max))
                link(dve.tensor_tensor(d, d, enm, ALU.max))
                link(dve.reciprocal(d, d))
                link(dve.tensor_tensor(v, d, d, ALU.mult))
                dve.tensor_tensor(v, v, ssum[0:L, first:end, :], ALU.mult).then_inc(var_ready, 1)

            def head_scale(r):
                first, end, L = ROUNDS[r]
                d, v = dd[0:L, first:end, :], hv[0:L, first:end, :]
                dve.wait_ge(root_done, r + 1)
                link(dve.reciprocal(v, v))
                dve.tensor_tensor(d, d, v, ALU.mult).then_inc(scale_ready, 1)

            for j in range(DT):
                middle, behind = IN_O[j]
                if middle and middle[0] == "out":
                    chunk(*middle)
                dve.wait_ge(unit_used, U_M + 17 + j + 1)
                scaled(og[:, j, :], 2 * ((17 + j) % 2)).then_inc(proj_read, 1)
                lo(U_M + RING + 17 + j)
                if behind:
                    chunk(*behind)
                if j in BEFORE_ROOT:
                    variance(BEFORE_ROOT.index(j))
                if j - 1 in BEFORE_ROOT:
                    head_scale(BEFORE_ROOT.index(j - 1))

            def y_low(j):
                dve.wait_ge(y_hi, j + 1)
                dve.tensor_tensor(u_lo[:, j, :], tmp[:, j % 2, :], f32(u_hi[:, j, :]), ALU.subtract) \
                    .then_inc(y_lo, 1)

            dve.wait_ge(m_out_done, 32)
            for j in range(DT):
                b = 4 + 2 * (j % 2)
                dve.wait_ge(y_psum, j + 1)
                dve.wait_ge(og_ready, j + 1)
                if j >= 2:
                    dve.wait_ge(y_lo, j - 1)
                dve.scalar_tensor_tensor(tmp[:, j % 2, 0:SEQ], ps[:, b, :], vecs[:, 2, j:j + 1],
                                         og[:, j, 0:SEQ], ALU.mult, ALU.mult)
                dve.scalar_tensor_tensor(tmp[:, j % 2, SEQ:TOK], ps[:, b + 1, 0:DEC_SEQ], vecs[:, 2, j:j + 1],
                                         og[:, j, SEQ:TOK], ALU.mult, ALU.mult).then_inc(y_read, 1)
                if j >= 1:
                    y_low(j - 1)
            y_low(DT - 1)
            for j in range(DT):
                if j == DT - 1:
                    for jj in range(DT - 2):
                        u_low(jj, 5, 4 * DT + jj + 1)
                dve.wait_ge(unit_used, U_MOUT + j + 1)
                dve.tensor_tensor(halves(x[:, j, :]), halves(x[:, j, :]), pair(2 * (j % 2)), ALU.add) \
                    .then_inc(x_ready, 1)
                if j < DT - 1:
                    lo(U_MOUT + RING + j)
            for j in (DT - 2, DT - 1):
                u_low(j, 5, 4 * DT + j + 1)
            lo(U_MOUT + RING + DT - 1)
            ffn(ffn_d, None, 0)

            rstd_cols(N_FINAL, 4)
            for c in range(NB):
                _, L = block_cols(c)
                col = c if c < NB - 1 else SAMPLE_COL
                dve.tensor_scalar(diag[0:L, c, 0:L], ident[0:L, 0:L], rms_col[0:L, col:col + 1],
                                  float(D_MODEL), ALU.mult, ALU.mult).then_inc(diag_ready, 1)
            dve.wait_ge(rstd_copied, 1)
            for j in range(N_POOL_OUT, DT):
                dve.scalar_tensor_tensor(x[:, j, :], x[:, j, :], gains[:, N_FINAL, j:j + 1], rstd[:, :],
                                         ALU.mult, ALU.mult).then_inc(out_tile, 1)

        @block.tensor
        def _(pe):
            def block_mm(n, kk, k, bank, first, last):
                w_h, w_l = (w[:, n % RING, kk * P:(kk + 1) * P] for w in (w_hi, w_lo))
                m_h, m_l = k
                for p, (w, m) in enumerate(((w_h, m_h), (w_h, m_l), (w_l, m_h))):
                    for h in range(2):
                        mm = pe.matmul(ps[:, bank + h, 0:HALF], w, m[:, h * HALF:(h + 1) * HALF],
                                       start=first and p == 0, stop=last and p == 2)
                return mm

            def u_tile(k):
                return u_hi[:, k, :], u_lo[:, k, :]

            def project(n, bank, i=0, ready=None, base=0, middle=None, each=None):
                pe.wait_ge(lo_split, n + 1 + RING * i)
                for k in range(DT):
                    if ready is not None:
                        pe.wait_ge(ready, base + k + 1)
                    mm = block_mm(n, k, u_tile(k), bank, k == 0, k == DT - 1)
                    if k == DT - 1:
                        mm.then_inc(unit_used, 1)
                    elif each is not None:
                        mm.then_inc(each, 1)
                    if k == 3 and middle:
                        middle()

            def norm(n):
                pe.wait_ge(sumsq_ready, n + 1)
                for h in range(2):
                    mm = pe.matmul(ps[:, 6 + h, 0:HALF], mean_w[:, :], sumsq[:, h * HALF:(h + 1) * HALF],
                                   start=True, stop=True)
                mm.then_inc(norm_psum, 1)

            def norm_cols(n):
                pe.wait_ge(sumsq_ready, n + 1)
                pe.wait_ge(sq_last, {N_POOL: 1, N_FINAL: 1}[n])
                for c in range(NB):
                    c0, L = block_cols(c)
                    col = c if c < NB - 1 else SAMPLE_COL
                    pe.matmul(ps[0:L, 5, col:col + 1], sumsq[:, c0:c0 + L], mean_w[:, 0:1],
                              start=True, stop=False)
                    mm = pe.matmul(ps[0:L, 5, col:col + 1], sq[:, c0:c0 + L], mean_w[:, 0:1],
                                   start=False, stop=True)
                mm.then_inc(norm_psum, 1)

            def project_two(n, bank, ready, base, ahead=None):
                for k in range(DT):
                    if ahead:
                        ahead(k)
                    pe.wait_ge(ready, base + k + 1)
                    for s in range(2):
                        if k == 0:
                            pe.wait_ge(lo_split, n + s + 1)
                        mm = block_mm(n + s, k, u_tile(k), bank + 2 * s, k == 0, k == DT - 1)
                        if k == DT - 1:
                            mm.then_inc(unit_used, 1)

            def ffn(f):
                for t in range(2):
                    if t == 0 and f.norm == 0:
                        project_two(f.base, 0, u_ready, 0)
                        norm(0)
                        continue
                    if t == 0:
                        pe.wait_ge(x_ready, DT * (f.norm + 1) - 1)
                    project(f.base + 2 * t, 4 * t, ready=u_ready if t == 0 else None, base=f.u_base)
                    if t == 0:
                        norm(f.norm)
                        pe.wait_ge(x_ready, DT * (f.norm + 1))
                    else:
                        pe.wait_ge(norm_root, f.norm + 1)
                    project(f.base + 2 * t + 1, 4 * t + 2)
                with pe.Fori(1, FT // 2) as i:
                    for t in range(2):
                        pe.wait_ge(f.psum_read, 2 * i + t - 1)
                        project(f.base + 2 * t, 4 * t, i)
                        project(f.base + 2 * t + 1, 4 * t + 2, i)
                with pe.Fori(0, DT // 4) as i:
                    for jj in range(4):
                        pe.wait_ge(f.psum_read, FT - 1)
                        pe.wait_ge(x_ready, DT * (f.norm + 1) + (4 * i + jj - 1 if jj else 3 * i))
                        k = 0
                        for s, size in enumerate(OUT_UNIT):
                            n = f.base + U_IN + 3 * jj + s
                            pe.wait_ge(lo_split, n + 1 + 3 * 4 * i)
                            for kk in range(size):
                                if jj == 0:
                                    pe.wait_ge(f.h_ready, k + 1)
                                mm = block_mm(n, kk, (h_hi[:, k, :], h_lo[:, k, :]), 2 * (jj % 2),
                                              k == 0, k == FT - 1)
                                k += 1
                            mm.then_inc(unit_used, 1)

            pe.wait_ge(mean_made, 1)
            for _ in range(18):
                pe.matmul(ps[:, 7, 0:P], mean_w[:, :], mean_w[:, :], start=True, stop=True)
            pe.wait_ge(consts_made, 2)
            ffn(ffn_a)

            pe.wait_ge(x_ready, 2 * DT)
            norm(N_POOL)
            for g in range(GROUPS):
                pe.wait_ge(lo_split, U_POOL + g + 1)
                pe.wait_ge(diff_lo, g + 1)
                for m in range(2):
                    j = 2 * g + m
                    if j >= 2:
                        pe.wait_ge(pool_y_ready, j - 1)
                    for k in range(2):
                        mm = block_mm(U_POOL + g, 2 * k + m, u_tile(2 * g + k), 2 * (j % 2), k == 0, k == 1)
                    mm.then_inc((pool_psum, unit_used)[m], 1)
            ffn(ffn_b)
            ffn(ffn_c)

            project(U_M, 4, ready=u_ready, base=3 * DT)
            norm(N_MIX)
            pe.wait_ge(x_ready, 5 * DT)
            for g in range(1, 9):
                if g > 2:
                    pe.wait_ge(proj_read, g)
                project(U_M + g, 2 * (g % 2))

            def item(kind, n, k):
                b = 4 + 2 * (k % 2)
                if k >= 2:
                    pe.wait_ge(*taken(k - 2))
                if k == 1:
                    pe.wait_ge(norm_root, N_MIX + 1)
                if kind == "cols":
                    pe.wait_ge(enm_row, 1)
                    pe.wait_ge(sel_made, 3)
                    for c in range(NB):
                        c0, L = block_cols(c)
                        for r, rows in enumerate((r_a, r_e)):
                            o = 16 * r + 4 * c if c < NB - 1 else 36 + 4 * r
                            pe.matmul(ps[0:L, b, o:o + 4], rows[:, c0:c0 + L], ident[0:4, 0:4],
                                      start=True, stop=True)
                    for h in range(HEADS):
                        mm = pe.matmul(ps[:, b, 32 + h:33 + h], sel[:, h, :], m_first[:, :],
                                       start=True, stop=True)
                elif kind == "mb":
                    for h in range(2):
                        mm = pe.matmul(ps[:, b + h, 0:HALF], sel[:, n, :], r_m[:, h * HALF:(h + 1) * HALF],
                                       start=True, stop=True)
                elif kind == "vt":
                    pe.wait_ge(proj_read, 10 + n + 1)
                    for c in range(NB - 1):
                        pe.transpose(ps[:, b, c * CH:(c + 1) * CH], og[:, n, c * CH:(c + 1) * CH], ident[:, :])
                    mm = pe.matmul(ps[0:DEC_SEQ, b + 1, 0:P], og[:, n, SEQ:TOK], ident[:, :],
                                   start=True, stop=True)
                elif kind == "sk":
                    c0, L = block_cols(n)
                    for h in range(HEADS):
                        k_c = k_t[:, h, c0:c0 + L]
                        pe.matmul(ps[0:L, b, h * L:(h + 1) * L], k_c, q_t[:, h, c0:c0 + L],
                                  start=True, stop=True)
                        if L == P:
                            mm = pe.transpose(ps[:, b + 1, h * P:(h + 1) * P], k_c, ident[:, :])
                        else:
                            mm = pe.matmul(ps[0:L, b + 1, h * P:(h + 1) * P], k_c, ident[:, :],
                                           start=True, stop=True)
                mm.then_inc(core_psum, 1)

            def chunk(kind, c):
                c0, L = block_cols(c)
                old, _ = old_state(c)
                if kind == "upd":
                    if c == 0:
                        pe.wait_ge(*taken(ITEM_AT[9] - 2))
                        pe.wait_ge(*taken(ITEM_AT[9] - 1))
                    else:
                        pe.wait_ge(out_read, c)
                    for h in range(HEADS):
                        mm = pe.matmul(ps[:, 4 + h, 0:DV + 1], k_w[0:L, c, h, :], v_one[0:L, c, h, :],
                                       start=True, stop=True)
                    mm.then_inc(upd_psum, 1)
                else:
                    pe.wait_ge(state_ready, c + 1)
                    if c:
                        pe.wait_ge(q_scaled, c)
                    if c == NB - 1:
                        pe.wait_ge(state_landed, 16)
                    for h in range(HEADS):
                        mm = pe.matmul(ps[0:L, 4 + h, 0:DV + 1], probs[0:L, h, c0:c0 + L],
                                       v_one[0:L, c, h, :], start=True, stop=c == 0)
                        if c:
                            mm = pe.matmul(ps[0:L, 4 + h, 0:DV + 1], q_t[:, h, c0:c0 + L],
                                           c_st[:, old, h, :], start=False, stop=True)
                    mm.then_inc(out_psum, 1)

            for t in range(DT):
                pe.wait_ge(proj_read, 9 + t)
                project(U_M + 9 + t, 2 * ((9 + t) % 2))
                for k, (kind, n) in enumerate(AFTER_V[t], ITEM_AT[t]):
                    item(kind, n, k)

            def in_o(what):
                if what and what[0] == "vt":
                    item("vt", 7, ITEM_AT[8])
                elif what:
                    chunk(*what)

            for j in range(DT):
                pe.wait_ge(proj_read, 17 + j)
                middle, behind = IN_O[j]
                project(U_M + 17 + j, 2 * ((17 + j) % 2), middle=lambda: in_o(middle))
                in_o(behind)
            pe.wait_ge(h_scaled, NB)

            def heads_back(j):
                b = 4 + 2 * (j % 2)
                h, d0 = j // 2, j % 2 * P
                if j >= 2:
                    pe.wait_ge(y_read, j - 1)
                for c in range(NB - 1):
                    pe.transpose(ps[:, b, c * CH:(c + 1) * CH], v_one[:, c, h, d0:d0 + P], ident[:, :])
                pe.matmul(ps[:, b + 1, 0:DEC_SEQ], v_one[0:DEC_SEQ, NB - 1, h, d0:d0 + P],
                          ident[0:DEC_SEQ, 0:DEC_SEQ], start=True, stop=True).then_inc(y_psum, 1)

            heads_back(0)
            heads_back(1)
            pe.wait_ge(proj_read, 26)
            project_two(U_MOUT, 0, y_lo, 0, ahead=lambda k: heads_back(k + 2) if k + 2 < DT else None)
            for j in range(2, DT):
                pe.wait_ge(x_ready, 5 * DT + j - 1)
                project(U_MOUT + j, 2 * (j % 2), each=u_free if j == DT - 1 else None)
            ffn(ffn_d)
            norm_cols(N_FINAL)
            for c in range(NB):
                c0, L = block_cols(c)
                pe.wait_ge(diag_ready, c + 1)
                t = c0
                while t < c0 + L:
                    h = t // HALF
                    e = min(c0 + L, (h + 1) * HALF)
                    mm = pe.matmul(ps[:, 6 + h, t - h * HALF:e - h * HALF], mean_w[0:L, :],
                                   diag[0:L, c, t - c0:e - c0], start=True, stop=True)
                    t = e
            mm.then_inc(spread, 1)


def _tiles(v):
    return v.reshape((DT, P) + v.shape[1:]).swapaxes(0, 1)


def kernel(x_prompt, x_sample, state_pool, state_mlstm_C, state_mlstm_n, state_mlstm_m, norm_ffn1,
           ffn1_w_in, ffn1_w_out, norm_mix, pool_w, pool_b, pool_scale, mlstm_w_in, mlstm_b_i, mlstm_b_f,
           mlstm_norm, mlstm_w_out, norm_ffn2, ffn2_w_in, ffn2_w_out, norm_final):
    import numpy as np
    import concourse.bacc as bacc
    from concourse.bass_utils import run_bass_kernel_spmd

    def ffn_in(w):
        return np.asarray(w).reshape(2, DT, P, 2, FT, P).transpose(0, 4, 3, 2, 1, 5).reshape(2, 2 * FT, P, DT * P)

    def ffn_out(w):
        return np.asarray(w).reshape(2, FT, P, DT, P).transpose(0, 3, 2, 1, 4).reshape(2, DT, P, FT * P)

    def square_w(w, n):
        return np.asarray(w).reshape(DT, P, n, P).transpose(2, 1, 0, 3).reshape(n, P, DT * P)

    w_mix = np.asarray(mlstm_w_in)[0]
    f1, mx, f2 = np.asarray(norm_ffn1), np.asarray(norm_mix), np.asarray(norm_ffn2)
    gains = np.stack([f1[0], mx[0], f2[0], f1[1], mx[1], f2[1], np.asarray(norm_final)], 1)
    vecs = np.stack([np.asarray(v)[0] for v in (pool_b, pool_scale, mlstm_norm)], 1)
    ins = {
        "x": _tiles(np.concatenate([np.asarray(x_prompt)[0], np.asarray(x_sample)[0]]).T),
        "pool_hist": _tiles(np.asarray(state_pool)[0, 0].T),
        "state_c": np.concatenate([np.asarray(state_mlstm_C)[0, 0].transpose(2, 0, 1),
                                   np.asarray(state_mlstm_n)[0, 0].T[:, :, None]], 2),
        "state_m": np.asarray(state_mlstm_m)[0, 0].reshape(HEADS, 1),
        "gains": _tiles(gains).transpose(0, 2, 1),
        "vecs": _tiles(vecs).transpose(0, 2, 1),
        "gate_b": np.stack([np.asarray(mlstm_b_i)[0], np.asarray(mlstm_b_f)[0]], 1),
        "ffn1_in": ffn_in(ffn1_w_in), "ffn1_out": ffn_out(ffn1_w_out),
        "ffn2_in": ffn_in(ffn2_w_in), "ffn2_out": ffn_out(ffn2_w_out),
        "pool_w": np.asarray(pool_w)[0].reshape(GROUPS, 2, P, 2 * P).transpose(0, 2, 1, 3).reshape(GROUPS, P, 4 * P),
        "mlstm_in": square_w(w_mix[:, :N_PROJ * P], N_PROJ),
        "mlstm_gates": _tiles(w_mix[:, N_PROJ * P:]).reshape(P, DT * 2 * HEADS),
        "mlstm_out": square_w(np.asarray(mlstm_w_out)[0], DT),
    }
    outs = {
        "y": (P, DT, TOK),
        "pool_prompt": (P, DT, HIST), "pool_sample": (P, DT, HIST),
        "c_prompt": (P, HEADS, DV + 1), "c_sample": (P, HEADS, DV + 1),
        "m_prompt": (HEADS, 1), "m_sample": (HEADS, 1),
    }
    nc = bacc.Bacc("TRN2", target_bir_lowering=False, num_devices=1)
    arrays, aps = {}, {}
    for name, v in ins.items():
        arrays["in_" + name] = np.ascontiguousarray(v)
        aps[name] = nc.dram_tensor("in_" + name, v.shape, mybir.dt.from_np(v.dtype), kind="ExternalInput").ap()
    for name, shape in outs.items():
        aps[name] = nc.dram_tensor("out_" + name, shape, mybir.dt.float32, kind="ExternalOutput").ap()
    encoder_step(nc, aps)
    got = run_bass_kernel_spmd(nc, [arrays], core_ids=[0]).results[0]
    r = {name: got["out_" + name] for name in outs}

    def rows(v):
        return np.ascontiguousarray(v.transpose(2, 1, 0).reshape(1, v.shape[2], D_MODEL))

    def state(v):
        return (np.ascontiguousarray(v[:, :, :DV].transpose(1, 2, 0))[None, None],
                np.ascontiguousarray(v[:, :, DV].T)[None, None])

    c_p, n_p = state(r["c_prompt"])
    c_s, n_s = state(r["c_sample"])
    return (rows(r["y"][:, :, :SEQ]), rows(r["y"][:, :, SEQ:]), rows(r["pool_prompt"])[None], c_p, n_p,
            r["m_prompt"].reshape(1, 1, HEADS), rows(r["pool_sample"])[None], c_s, n_s,
            r["m_sample"].reshape(1, 1, HEADS))
```

```python
import concourse.bass as bass
from concourse import mybir

P = 128
D_MODEL = 1024
DT = D_MODEL // P
SEQ, DEC_SEQ = 512, 64
TOK = SEQ + DEC_SEQ
HALF = TOK // 2
D_FF = 2816
FT = D_FF // P
HIST = 15
GROUPS = 4
IN, NEXT, START, LAST, BAND = 0, 128, 128 + HIST, 128 + 2 * HIST, 128 + 2 * HIST + DEC_SEQ
HEADS = 4
DV = 256
CH = 128
NB = SEQ // CH + 1
EPS = 1e-6
RING, RAW = 4, 2

U_IN, U_OUT = 2 * FT, 3 * DT
FFN_UNITS = U_IN + U_OUT
U_A = 0
U_POOL = U_A + FFN_UNITS
U_B = U_POOL + GROUPS
U_C = U_B + FFN_UNITS
U_M = U_C + FFN_UNITS
N_PROJ = 3 * DT
U_MOUT = U_M + 1 + N_PROJ
U_D = U_MOUT + DT
U_END = U_D + FFN_UNITS
OUT_UNIT = (8, 8, 6)


def unit_blocks(n):
    for start in (U_A, U_B, U_C, U_D):
        if start + U_IN <= n < start + FFN_UNITS:
            return OUT_UNIT[(n - start - U_IN) % 3]
    if U_POOL <= n < U_B:
        return 4
    return 8


def encoder_step(nc, a):
    F32, F32R = mybir.dt.float32, mybir.dt.float32r
    ALU, ACT = mybir.AluOpType, mybir.ActivationFunctionType

    place = [(nc.sbuf_base + 63) // 64 * 64]

    def sb(name, shape, dt=F32, at=None):
        size = 4
        for s in shape[1:]:
            size *= s
        offset = place[0] if at is None else at
        if at is None:
            place[0] += (size + 31) // 32 * 32
        return nc.alloc_sbuf_tensor_at(name, shape, dt, offset=offset)

    x = sb("x", [P, DT, TOK])
    u_hi, u_lo = sb("u_hi", [P, DT, TOK + HIST], F32R), sb("u_lo", [P, DT, TOK + HIST], F32R)
    scratch = place[0]
    h_hi, h_lo = sb("h_hi", [P, FT, TOK], F32R), sb("h_lo", [P, FT, TOK], F32R)
    scratch_end = place[0]
    w_raw = sb("w_raw", [P, RAW, 8 * P])
    w_hi, w_lo = sb("w_hi", [P, RING, 8 * P], F32R), sb("w_lo", [P, RING, 8 * P], F32R)
    rstd = sb("rstd", [P, TOK])
    rows_at = place[0]
    tmp = sb("tmp", [P, 2, TOK])
    sumsq, sq = sb("sumsq", [P, TOK]), sb("sq", [P, TOK])
    gains = sb("gains", [P, 7, DT])
    vecs = sb("vecs", [P, 3, DT])
    pool_bs = sb("pool_bs", [P, DT])
    mean_w = sb("mean_w", [P, P])
    warm = sb("warm", [P, 1])
    rms_col = sb("rms_col", [P, 40])
    ident = sb("ident", [P, P])
    eps_col, one_col = sb("eps_col", [P, 1]), sb("one_col", [P, 1])
    gate_b, m_first = sb("gate_b", [4, 2]), sb("m_first", [4, 1])
    cols = sb("cols", [P, 44])
    mend = sb("mend", [P, 6, HEADS])
    w_write = sb("w_write", [P, NB, HEADS])
    carry = sb("carry", [P, 4, HEADS])
    ssum = sb("ssum", [P, NB, HEADS])
    dd, hv = sb("dd", [P, NB, HEADS]), sb("hv", [P, NB, HEADS])
    assert place[0] <= nc.sbuf_usable_end, place[0]

    cursor = [scratch]

    def over(name, shape):
        size = 4
        for s in shape[1:]:
            size *= s
        offset = cursor[0]
        cursor[0] += (size + 31) // 32 * 32
        assert cursor[0] <= scratch_end, name
        return sb(name, shape, at=offset)

    z = over("z", [P, GROUPS, NB, 2 * P])
    pool_y = over("pool_y", [P, 2, TOK])
    state = over("state", [P, 2, DT, HIST])
    bands = sb("bands", [P, GROUPS, BAND], at=rows_at)

    cursor[0] = scratch
    q_t = over("q_t", [P, HEADS, TOK])
    junk = sb("junk", [P, DV], at=cursor[0])
    k_t = over("k_t", [P, HEADS, TOK])
    v_one = over("v_one", [P, NB, HEADS, DV + 1])
    k_w = over("k_w", [P, NB, HEADS, P])
    og = over("og", [P, DT, TOK])
    m_b = over("m_b", [P, HEADS, TOK])
    probs = over("probs", [P, HEADS, TOK])
    c_st = over("c_st", [P, 3, HEADS, DV + 1])
    sel = over("sel", [4, HEADS, P])
    later = over("later", [P, P])

    cursor[0] = scratch
    diag = over("diag", [P, NB, P])
    hist = sb("hist", [P, DT, HIST], at=scratch)
    assert GROUPS * BAND <= 2 * TOK
    row = [sb(f"row{n}", [4, TOK], at=rows_at + n * TOK * 4) for n in range(4)]
    r_a, r_f, r_e, r_m = row

    ps = nc.alloc_psum_tensor("ps", [P, 8, 512], F32)

    def pair(b):
        return ps[:, b:b + 2, 0:HALF]

    def halves(ap):
        return ap.rearrange("p (h n) -> p h n", h=2)

    def f32(ap):
        return ap.bitcast(F32)

    sem = nc.alloc_semaphore
    raw_landed = [sem(f"raw_landed{s}") for s in range(RAW)]
    hi_split, lo_split, unit_used = sem("hi_split"), sem("lo_split"), sem("unit_used")
    x_landed = [sem(f"x_landed{j}") for j in range(DT)]
    gains_landed, consts_landed = sem("gains_landed"), sem("consts_landed")
    mean_made, consts_made = sem("mean_made"), sem("consts_made")
    x_ready = sem("x_ready")
    u_hi_ready, u_ready = sem("u_hi_ready"), sem("u_ready")
    sq_step, sumsq_ready = sem("sq_step"), sem("sumsq_ready")
    sq_last = sem("sq_last")
    norm_psum, norm_root, rstd_ready = sem("norm_psum"), sem("norm_root"), sem("rstd_ready")
    diag_ready, spread, rstd_copied = sem("diag_ready"), sem("spread"), sem("rstd_copied")
    dve_order = sem("dve_order")
    stores = sem("stores")

    class Ffn:
        def __init__(self, name, base, norm, u_base, w_in, w_out):
            self.base, self.norm, self.u_base, self.w_in, self.w_out = base, norm, u_base, w_in, w_out
            self.gate_scaled = sem(name + "_gate_scaled")
            self.silu_done = sem(name + "_silu_done")
            self.mul_done = sem(name + "_mul_done")
            self.psum_read = sem(name + "_psum_read")
            self.h_hi_ready = sem(name + "_h_hi_ready")
            self.h_ready = sem(name + "_h_ready")

    ffn_a = Ffn("a", U_A, 0, 0, a["ffn1_in"][0], a["ffn1_out"][0])
    ffn_b = Ffn("b", U_B, 2, 16, a["ffn2_in"][0], a["ffn2_out"][0])
    ffn_c = Ffn("c", U_C, 3, 24, a["ffn1_in"][1], a["ffn1_out"][1])
    ffn_d = Ffn("d", U_D, 5, 40, a["ffn2_in"][1], a["ffn2_out"][1])
    N_POOL, N_MIX, N_FINAL = 1, 4, 6
    N_POOL_OUT = 2

    hist_hi, hist_lo, bands_landed = sem("hist_hi"), sem("hist_lo"), sem("bands_landed")
    z_dve, z_act = sem("z_dve"), sem("z_act")
    state_step, state_made = sem("state_step"), sem("state_made")
    pool_psum, pool_y_ready = sem("pool_psum"), sem("pool_y_ready")
    pool_out_done, m_out_done, c_out_done = sem("pool_out_done"), sem("m_out_done"), sem("c_out_done")
    state_landed, sel_made = sem("state_landed"), sem("sel_made")
    proj_read = sem("proj_read")
    gate_abs, gate_exp, gate_log = sem("gate_abs"), sem("gate_exp"), sem("gate_log")
    rows_ready, enm_row = sem("rows_ready"), sem("enm_row")
    core_psum, dve_took, act_took = sem("core_psum"), sem("dve_took"), sem("act_took")
    ends_ready, factors_ready = sem("ends_ready"), sem("factors_ready")
    expo_ready, expo_done = sem("expo_ready"), sem("expo_done")
    q_factor, q_scaled = sem("q_factor"), sem("q_scaled")
    upd_psum, state_ready = sem("upd_psum"), sem("state_ready")
    out_psum, out_read = sem("out_psum"), sem("out_read")
    act_order, squares = sem("act_order"), sem("squares")
    var_ready, root_done, scale_ready, h_scaled = (
        sem("var_ready"), sem("root_done"), sem("scale_ready"), sem("h_scaled"))
    og_ready, u_free = sem("og_ready"), sem("u_free")
    y_psum, y_read, y_hi, y_lo = sem("y_psum"), sem("y_read"), sem("y_hi"), sem("y_lo")
    out_tile, out_pool = sem("out_tile"), sem("out_pool")

    SAMPLE_COL = 39

    def block_cols(c):
        return c * CH, (CH if c < NB - 1 else DEC_SEQ)

    def z_place(g, c, rows):
        bank = 2 if c == NB - 1 else 3 * (g % 2) + c // 2
        return ps[0:rows, bank, 2 * P * (c % 2):2 * P * (c % 2 + 1)]

    FIRST_UNITS = [0, 4, 6]
    AFTER_V = [[("cols", 0), ("mb", 0)], [("mb", 1), ("mb", 2)], [("mb", 3), ("vt", 0)],
               [("vt", 1), ("sk", 0)], [("vt", 2), ("sk", 1)], [("vt", 3), ("sk", 2)],
               [("vt", 4), ("vt", 5), ("sk", 3)], [("vt", 6), ("sk", 4)], [("vt", 7)]]
    ITEM_AT = [sum(map(len, AFTER_V[:t])) for t in range(10)]
    ALL_ITEMS = sum(AFTER_V, [])

    def taken(k):
        on_dve = [kind in ("cols", "sk") for kind, _ in ALL_ITEMS[:k + 1]]
        return (dve_took, sum(on_dve)) if on_dve[k] else (act_took, k + 1 - sum(on_dve))

    IN_O = [(("vt", 7), ("upd", 0)), (("out", 0), ("upd", 1)), (("out", 1), ("upd", 2)),
            (("out", 2), ("upd", 3)), (("out", 3), ("upd", 4)), (("out", 4), None),
            (None, None), (None, None)]
    ROUNDS = [(0, 2, CH), (2, 4, CH), (4, 5, DEC_SEQ)]
    BEFORE_ROOT = [2, 4, 5]

    def old_state(c):
        return (1, 0) if c == NB - 1 else (2 * ((c + 1) % 2), 2 * (c % 2))

    block = nc.Block()
    with block as block:

        @block.sync
        def _(sp):
            def load(n, src, i=0, step=0):
                if n >= RAW:
                    sp.wait_ge(lo_split, n - RAW + 1 + step * i)
                sp.dma_start(w_raw[:, n % RAW, 0:src.shape[1]], src).then_inc(raw_landed[n % RAW], 16)

            def load_ffn(f, first=0):
                for n in range(first):
                    load(f.base + n, f.w_in[n, :, :])
                if first:
                    for j in range(2, DT):
                        sp.dma_start(x[:, j, :], a["x"][:, j, :]).then_inc(x_landed[j], 16)
                with sp.Fori(first // 2, FT) as i:
                    for s in range(2):
                        sp.wait_ge(lo_split, f.base + s - RAW + 1 + 2 * i)
                        slot = (f.base + s) % RAW
                        sp.dma_start(w_raw[:, slot, :], f.w_in[2 * i + s, :, :]) \
                            .then_inc(raw_landed[slot], 16)
                with sp.Fori(0, DT // 2) as i:
                    for jj in range(2):
                        k = 0
                        for s, size in enumerate(OUT_UNIT):
                            n = f.base + U_IN + 3 * jj + s
                            sp.wait_ge(lo_split, n - RAW + 1 + 6 * i)
                            sp.dma_start(w_raw[:, n % RAW, 0:size * P],
                                         f.w_out[2 * i + jj, :, k * P:(k + size) * P]) \
                                .then_inc(raw_landed[n % RAW], 16)
                            k += size

            load_ffn(ffn_a, first=2)
            sp.wait_ge(ffn_a.h_ready, FT)
            sp.dma_start(bands[:, :, :], a["bands"]).then_inc(bands_landed, 16)
            for g in range(GROUPS):
                load(U_POOL + g, a["pool_w"][g, :, :])
            load_ffn(ffn_b)
            load_ffn(ffn_c)
            load(U_M, a["mlstm_gates"])
            with sp.Fori(0, N_PROJ // 2) as i:
                for s in range(2):
                    n = U_M + 1 + s
                    sp.wait_ge(lo_split, n - RAW + 1 + 2 * i)
                    sp.dma_start(w_raw[:, n % RAW, :], a["mlstm_in"][2 * i + s, :, :]) \
                        .then_inc(raw_landed[n % RAW], 16)
            with sp.Fori(0, DT // 2) as i:
                for s in range(2):
                    n = U_MOUT + s
                    sp.wait_ge(lo_split, n - RAW + 1 + 2 * i)
                    sp.dma_start(w_raw[:, n % RAW, :], a["mlstm_out"][2 * i + s, :, :]) \
                        .then_inc(raw_landed[n % RAW], 16)
            load_ffn(ffn_d)
            for j in (2, 3, 0, 4, 5, 1, 6, 7):
                if j < N_POOL_OUT:
                    sp.wait_ge(out_pool, j + 1)
                else:
                    sp.wait_ge(out_tile, j - N_POOL_OUT + 1)
                sp.dma_start(a["y"][:, j, :], x[:, j, :]).then_inc(stores, 16)
            sp.wait_ge(stores, 16 * DT)

        @block.gpsimd
        def _(pool):
            pool.memset(mean_w[:, :], 1.0 / D_MODEL).then_inc(mean_made, 1)
            pool.dma_start(vecs[:, :, :], a["vecs"]).then_inc(consts_landed, 16)
            pool.dma_start(gate_b[:, :], a["gate_b"]).then_inc(consts_landed, 16)
            pool.dma_start(m_first[:, :], a["state_m"]).then_inc(consts_landed, 16)
            pool.dma_start(hist[:, :, :], a["pool_hist"]).then_inc(consts_landed, 16)
            pool.memset(eps_col[:, :], EPS)
            pool.memset(one_col[:, :], 1.0)
            pool.memset(ident[:, :], 0.0)
            pool.memset(dd[:, :, :], 0.0).then_inc(consts_made, 1)
            pool.wait_ge(consts_made, 1)
            pool.affine_select(out=ident[:, :], in_=ident[:, :], compare_op=ALU.not_equal, fill=1.0,
                               base=0, pattern=[[-1, P]], channel_multiplier=1).then_inc(consts_made, 1)

            steps = [0]

            def square(j, last=DT - 1):
                if j == 0:
                    pool.tensor_tensor(sumsq[:, :], x[:, j, :], x[:, j, :], ALU.mult).then_inc(sq_step, 1)
                    steps[0] += 1
                    return
                pool.wait_ge(sq_step, steps[0])
                pool.tensor_tensor(sq[:, :], x[:, j, :], x[:, j, :], ALU.mult).then_inc(sq_step, 1)
                steps[0] += 1
                pool.wait_ge(sq_step, steps[0])
                add = pool.tensor_tensor(sumsq[:, :], sumsq[:, :], sq[:, :], ALU.add)
                if j < last:
                    add.then_inc(sq_step, 1)
                    steps[0] += 1
                else:
                    add.then_inc(sumsq_ready, 1)

            def squares_after(norm, tiles=DT):
                pool.wait_ge(norm_psum, norm)
                for j in range(tiles):
                    pool.wait_ge(x_ready, DT * norm + j + 1)
                    square(j, tiles - 1)

            for j in range(DT):
                pool.wait_ge(x_landed[j], 16)
                square(j)
            squares_after(1, DT - 1)

            pool.wait_ge(rstd_ready, N_POOL + 1)
            for s, end in enumerate((SEQ, TOK)):
                pool.tensor_tensor(state[:, s, :, :], x[:, :, end - HIST:end],
                                   rms_col[:, 4 + HIST * s:4 + HIST * (s + 1)].unsqueeze(1)
                                   .to_broadcast([P, DT, HIST]), ALU.mult).then_inc(state_step, 1)
            pool.wait_ge(state_step, 2)
            for s in range(2):
                last = pool.tensor_tensor(state[:, s, :, :], state[:, s, :, :],
                                          gains[:, N_POOL, :].unsqueeze(2).to_broadcast([P, DT, HIST]), ALU.mult)
            last.then_inc(state_made, 1)
            pool.wait_ge(state_made, 1)
            for s, name in enumerate(("pool_prompt", "pool_sample")):
                pool.dma_start(a[name], state[:, s, :, :]).then_inc(pool_out_done, 16)
            squares_after(2)
            squares_after(3)
            squares_after(4)

            pool.wait_ge(norm_psum, N_MIX + 1)
            pool.memset(later[:, :], 0.0)
            pool.memset(sel[:, :, :], 0.0).then_inc(sel_made, 1)
            pool.wait_ge(sel_made, 1)
            pool.affine_select(out=sel[:, :, :], in_=sel[:, :, :], compare_op=ALU.not_equal, fill=1.0,
                               base=0, pattern=[[-1, HEADS], [0, P]], channel_multiplier=1) \
                .then_inc(sel_made, 1)
            pool.affine_select(out=later[:, :], in_=later[:, :], compare_op=ALU.is_ge, fill=1e30,
                               base=0, pattern=[[1, P]], channel_multiplier=-1)
            pool.memset(v_one[:, :, :, DV:DV + 1], 1.0).then_inc(sel_made, 1)
            for c in range(NB):
                _, n = block_cols(c)
                pool.wait_ge(scale_ready, c // 2 + 1)
                pool.tensor_tensor(v_one[0:n, c, :, 0:DV], v_one[0:n, c, :, 0:DV],
                                   dd[0:n, c, :].unsqueeze(2).to_broadcast([n, HEADS, DV]), ALU.mult) \
                    .then_inc(h_scaled, 1)
            squares_after(5)
            squares_after(6, DT - 1)
            for j in range(N_POOL_OUT):
                pool.wait_ge(rstd_copied, 1)
                pool.tensor_tensor(x[:, j, :], tmp[:, j, :], rstd[:, :], ALU.mult).then_inc(out_pool, 1)

        @block.scalar
        def _(act):
            act.dma_start(x[:, 0, :], a["x"][:, 0, :]).then_inc(x_landed[0], 16)
            act.dma_start(gains[:, :, :], a["gains"]).then_inc(gains_landed, 16)
            act.dma_start(x[:, 1, :], a["x"][:, 1, :]).then_inc(x_landed[1], 16)
            act.wait_ge(mean_made, 1)
            act.activation(warm[:, :], mean_w[:, 0:1], ACT.Copy)

            def hi(n, i=0):
                size = unit_blocks(n) * P
                if n >= U_END:
                    return
                act.wait_ge(raw_landed[n % RAW], 16 * (n // RAW + 1) + 32 * i)
                if n >= RING:
                    act.wait_ge(unit_used, n - RING + 1 + RING * i)
                if n == U_M:
                    src = w_raw[:, n % RAW, 0:64].rearrange("p (k g c) -> p k g c", k=8, g=2)
                    dst = w_hi[:, n % RING, :].rearrange("p (k g c) -> p k g c", k=8, g=4)
                    act.activation(dst[:, :, 0:2, 0:4], src, ACT.Copy).then_inc(hi_split, 1)
                else:
                    act.activation(w_hi[:, n % RING, 0:size], w_raw[:, n % RAW, 0:size], ACT.Copy) \
                        .then_inc(hi_split, 1)

            def u_high(j, norm):
                act.activation(u_hi[:, j, 0:TOK], x[:, j, :], ACT.Copy, scale=gains[:, norm, j:j + 1]) \
                    .then_inc(u_hi_ready, 1)

            def root(norm):
                act.wait_ge(norm_psum, norm + 1)
                act.activation(halves(rstd[:, :]), pair(6), ACT.Sqrt, bias=eps_col[:, :]) \
                    .then_inc(norm_root, 1)

            def last_square(norm):
                act.activation(warm[:, :], eps_col[:, :], ACT.Sqrt)
                act.wait_ge(sumsq_ready, norm + 1)
                act.wait_ge(x_ready, DT * (norm + 1))
                act.activation(sq[:, :], x[:, DT - 1, :], ACT.Square).then_inc(sq_last, 1)

            def root_cols(norm, n):
                act.wait_ge(norm_psum, norm + 1)
                act.activation(rms_col[:, 0:n], ps[:, 5, 0:n], ACT.Sqrt, bias=eps_col[:, :])
                act.activation(rms_col[0:DEC_SEQ, SAMPLE_COL:SAMPLE_COL + 1],
                               ps[0:DEC_SEQ, 5, SAMPLE_COL:SAMPLE_COL + 1], ACT.Sqrt,
                               bias=eps_col[0:DEC_SEQ, :]).then_inc(norm_root, 1)

            def ffn(f, next_norm):
                root(f.norm)

                def tile(n, t, i):
                    hi(n, i)
                    act.wait_ge(f.gate_scaled, 2 * i + t + 1)
                    act.activation(tmp[:, t, :], tmp[:, t, :], ACT.Silu).then_inc(f.silu_done, 1)
                    hi(n + 1, i)
                    act.wait_ge(f.psum_read, 2 * i + t + 1)
                    act.activation(h_hi[:, 2 * i + t, :], tmp[:, t, :], ACT.Copy) \
                        .then_inc(f.h_hi_ready, 1)

                with act.Fori(0, FT // 2 - 1) as i:
                    for t in range(2):
                        tile(f.base + RING + 2 * t, t, i)
                for t in range(2):
                    act_i = FT // 2 - 1
                    n = f.base + RING + 2 * t + RING * act_i
                    hi(n)
                    act.wait_ge(f.gate_scaled, 2 * act_i + t + 1)
                    act.activation(tmp[:, t, :], tmp[:, t, :], ACT.Silu).then_inc(f.silu_done, 1)
                    hi(n + 1)
                    act.wait_ge(f.psum_read, 2 * act_i + t + 1)
                    act.activation(h_hi[:, 2 * act_i + t, :], tmp[:, t, :], ACT.Copy) \
                        .then_inc(f.h_hi_ready, 1)
                for j in range(DT):
                    n = f.base + U_IN + 3 * j + RING
                    hi(n)
                    hi(n + 1)
                    if next_norm is not None:
                        act.wait_ge(x_ready, DT * (f.norm + 1) + j + 1)
                        u_high(j, next_norm)
                    hi(n + 2)

            hi(0)
            act.wait_ge(gains_landed, 16)
            for j in range(DT):
                act.wait_ge(x_landed[j], 16)
                u_high(j, 0)
                if j in FIRST_UNITS:
                    hi(FIRST_UNITS.index(j) + 1)
            act.wait_ge(consts_landed, 64)
            act.activation(u_hi[:, :, TOK:TOK + HIST], hist[:, :, :], ACT.Copy).then_inc(hist_hi, 1)
            act.wait_ge(consts_made, 2)
            ffn(ffn_a, N_POOL)

            last_square(N_POOL)
            root_cols(N_POOL, 4 + 2 * HIST)
            def pool_out(g):
                for m in range(2):
                    j = 2 * g + m
                    if m == 0:
                        act.wait_ge(pool_psum, 2 * g + 1)
                    else:
                        act.wait_ge(pool_psum, 2 * g + 2)
                    if j >= 2:
                        act.wait_ge(x_ready, 2 * DT + j - 1)
                    act.activation(pool_y[:, m, 0:SEQ], ps[:, 6 + m, :], ACT.Identity,
                                   scale=vecs[:, 1, j:j + 1], bias=pool_bs[:, j:j + 1])
                    act.activation(pool_y[:, m, SEQ:TOK], ps[:, 5, 0:DEC_SEQ], ACT.Identity,
                                   scale=vecs[:, 1, j:j + 1], bias=pool_bs[:, j:j + 1]) \
                        .then_inc(pool_y_ready, 1)
                for m in range(2):
                    act.wait_ge(x_ready, 2 * DT + 2 * g + m + 1)
                    u_high(2 * g + m, 2)
                hi(U_B + g)

            act.wait_ge(rstd_ready, N_POOL + 1)
            for g in range(GROUPS):
                act.wait_ge(unit_used, U_POOL + g + 1)
                act.activation(z[0:DEC_SEQ, g, 4, :], z_place(g, 4, DEC_SEQ), ACT.Copy,
                               scale=rms_col[0:DEC_SEQ, SAMPLE_COL:SAMPLE_COL + 1])
                act.activation(z[DEC_SEQ:DEC_SEQ + HIST, g, 4, :],
                               z_place(g, 4, DEC_SEQ + HIST)[DEC_SEQ:DEC_SEQ + HIST, :], ACT.Copy)
                for c in (2, 3):
                    last = act.activation(z[:, g, c, :], z_place(g, c, P), ACT.Copy,
                                          scale=rms_col[:, c:c + 1])
                last.then_inc(z_act, 1)
                if g >= 2:
                    pool_out(g - 2)
            pool_out(GROUPS - 2)
            pool_out(GROUPS - 1)
            act.wait_ge(pool_out_done, 32)
            ffn(ffn_b, 3)
            ffn(ffn_c, 4)

            root(N_MIX)
            act.dma_start(c_st[:, 1, :, :], a["state_c"]).then_inc(state_landed, 16)
            hi(U_M + RING)
            for g in range(1, 9):
                if g == 1:
                    act.wait_ge(gate_abs, 1)
                    act.activation(r_e[:, :], r_e[:, :], ACT.Exp, scale=-1.0).then_inc(gate_exp, 1)
                    act.wait_ge(gate_exp, 1)
                    act.activation(r_e[:, :], r_e[:, :], ACT.Ln, bias=one_col[0:4, :]).then_inc(gate_log, 1)
                if g == 5:
                    act.wait_ge(rows_ready, 1)
                    act.activation(r_e[:, :], r_f[:, :], ACT.Exp, scale=-1.0).then_inc(enm_row, 1)
                    act.dma_start(a["m_prompt"], r_f[:, SEQ - 1:SEQ]).then_inc(m_out_done, 16)
                    act.dma_start(a["m_sample"], r_f[:, TOK - 1:TOK]).then_inc(m_out_done, 16)
                hi(U_M + RING + g)

            def item(kind, n, k):
                b = 4 + 2 * (k % 2)
                if kind == "mb":
                    act.wait_ge(core_psum, k + 1)
                    act.activation(halves(m_b[:, n, :]), pair(b), ACT.Copy).then_inc(act_took, 1)
                elif kind == "vt":
                    act.wait_ge(core_psum, k + 1)
                    h, d0 = n // 2, n % 2 * P
                    act.activation(v_one[:, 0:NB - 1, h, d0:d0 + P],
                                   ps[:, b, :].rearrange("p (c d) -> p c d", c=NB - 1), ACT.Copy)
                    act.activation(v_one[0:DEC_SEQ, NB - 1, h, d0:d0 + P], ps[0:DEC_SEQ, b + 1, 0:P],
                                   ACT.Copy).then_inc(act_took, 1)
                elif kind == "sk":
                    c0, L = block_cols(n)
                    if n == 0:
                        act.wait_ge(ends_ready, 1)
                        act.activation(w_write[:, 0:NB - 1, :], w_write[:, 0:NB - 1, :], ACT.Exp)
                        act.activation(w_write[0:DEC_SEQ, NB - 1, :], w_write[0:DEC_SEQ, NB - 1, :], ACT.Exp)
                        act.activation(carry[:, :, :], carry[:, :, :], ACT.Exp).then_inc(factors_ready, 1)
                    act.wait_ge(expo_ready, n + 1)
                    act.activation(probs[0:L, :, c0:c0 + L], probs[0:L, :, c0:c0 + L], ACT.Exp, scale=-1.0) \
                        .then_inc(expo_done, 1)
                    if n >= 1:
                        before = n - 1 if n < NB - 1 else 4
                        for h in range(HEADS):
                            last = act.activation(m_b[:, h, c0:c0 + L], m_b[:, h, c0:c0 + L], ACT.Exp,
                                                  scale=-1.0, bias=mend[:, before, h:h + 1])
                        last.then_inc(q_factor, 1)

            for t in range(DT):
                hi(U_M + RING + 9 + t)
                for k, (kind, n) in enumerate(AFTER_V[t], ITEM_AT[t]):
                    item(kind, n, k)
            order = 0
            for j in range(DT):
                middle, _ = IN_O[j]
                if middle and middle[0] == "vt":
                    item("vt", 7, ITEM_AT[8])
                elif middle:
                    c = middle[1]
                    _, L = block_cols(c)
                    act.wait_ge(out_read, c + 1)
                    for h in range(HEADS):
                        last = act.activation(junk[0:L, :], v_one[0:L, c, h, 0:DV], ACT.Square,
                                              accum_out=ssum[0:L, c, h:h + 1])
                        if h < HEADS - 1:
                            last.then_inc(act_order, 1)
                            order += 1
                            act.wait_ge(act_order, order)
                    last.then_inc(squares, 1)
                if j - 1 in BEFORE_ROOT:
                    r = BEFORE_ROOT.index(j - 1)
                    first, end, L = ROUNDS[r]
                    act.wait_ge(var_ready, r + 1)
                    act.activation(hv[0:L, first:end, :], hv[0:L, first:end, :], ACT.Sqrt,
                                   scale=1.0 / DV, bias=eps_col[0:L, :]).then_inc(root_done, 1)
                hi(U_M + RING + 17 + j)
                act.wait_ge(proj_read, 18 + j + 1)
                act.activation(og[:, j, :], og[:, j, :], ACT.Sigmoid).then_inc(og_ready, 1)
            act.wait_ge(state_ready, NB)
            act.dma_start(a["c_prompt"], c_st[:, 2, :, :]).then_inc(c_out_done, 16)
            act.dma_start(a["c_sample"], c_st[:, 0, :, :]).then_inc(c_out_done, 16)
            for j in range(DT):
                act.wait_ge(y_read, j + 1)
                act.activation(u_hi[:, j, 0:TOK], tmp[:, j % 2, :], ACT.Copy).then_inc(y_hi, 1)
            for j in range(DT - 1):
                hi(U_MOUT + RING + j)
            for j in range(DT):
                if j < DT - 1:
                    act.wait_ge(u_free, j + 1)
                act.wait_ge(x_ready, 5 * DT + j + 1)
                u_high(j, 5)
            hi(U_MOUT + RING + DT - 1)
            act.wait_ge(c_out_done, 32)
            ffn(ffn_d, None)
            for j in range(N_POOL_OUT):
                act.activation(tmp[:, j, :], x[:, j, :], ACT.Copy, scale=gains[:, N_FINAL, j:j + 1])
            last_square(N_FINAL)
            root_cols(N_FINAL, 4)
            act.wait_ge(spread, 1)
            act.activation(halves(rstd[:, :]), pair(6), ACT.Copy).then_inc(rstd_copied, 1)

        @block.vector
        def _(dve):
            order = [0]

            def link(ins):
                order[0] += 1
                ins.then_inc(dve_order, 1)
                dve.wait_ge(dve_order, order[0])

            def lo(n, i=0):
                size = unit_blocks(n) * P
                if n >= U_END:
                    return
                dve.wait_ge(hi_split, n + 1 + RING * i)
                if n == U_M:
                    src = w_raw[:, n % RAW, 0:64].rearrange("p (k g c) -> p k g c", k=8, g=2)
                    parts = [w[:, n % RING, :].rearrange("p (k g c) -> p k g c", k=8, g=4)[:, :, 0:2, 0:4]
                             for w in (w_hi, w_lo)]
                    dve.tensor_tensor(parts[1], src, f32(parts[0]), ALU.subtract).then_inc(lo_split, 1)
                else:
                    dve.tensor_tensor(w_lo[:, n % RING, 0:size], w_raw[:, n % RAW, 0:size],
                                      f32(w_hi[:, n % RING, 0:size]), ALU.subtract).then_inc(lo_split, 1)

            def u_low(j, norm, count):
                dve.wait_ge(u_hi_ready, count)
                dve.scalar_tensor_tensor(u_lo[:, j, 0:TOK], x[:, j, :], gains[:, norm, j:j + 1],
                                         f32(u_hi[:, j, 0:TOK]), ALU.mult, ALU.subtract).then_inc(u_ready, 1)

            def rstd_of(norm):
                dve.wait_ge(norm_root, norm + 1)
                dve.reciprocal(rstd[:, :], rstd[:, :]).then_inc(rstd_ready, 1)
                dve.wait_ge(rstd_ready, norm + 1)

            def rstd_cols(norm, n):
                dve.wait_ge(norm_root, norm + 1)
                dve.reciprocal(rms_col[:, 0:n], rms_col[:, 0:n])
                dve.reciprocal(rms_col[0:DEC_SEQ, SAMPLE_COL:SAMPLE_COL + 1],
                               rms_col[0:DEC_SEQ, SAMPLE_COL:SAMPLE_COL + 1]).then_inc(rstd_ready, 1)
                dve.wait_ge(rstd_ready, norm + 1)

            def scaled(dst, bank):
                return dve.tensor_tensor(halves(dst), pair(bank), halves(rstd[:, :]), ALU.mult)

            def ffn(f, next_norm, next_u):
                rstd_of(f.norm)

                def tile(t, i, ahead):
                    used = f.base + 2 * t + RING * i
                    dve.wait_ge(unit_used, used + 1)
                    scaled(tmp[:, t, :], 4 * t).then_inc(f.gate_scaled, 1)
                    ahead(0)
                    dve.wait_ge(f.silu_done, 2 * i + t + 1)
                    dve.tensor_tensor(tmp[:, t, :], tmp[:, t, :], rstd[:, :], ALU.mult) \
                        .then_inc(f.mul_done, 1)
                    dve.wait_ge(f.mul_done, 2 * i + t + 1)
                    dve.wait_ge(unit_used, used + 2)
                    dve.tensor_tensor(halves(tmp[:, t, :]), halves(tmp[:, t, :]), pair(4 * t + 2), ALU.mult) \
                        .then_inc(f.psum_read, 1)
                    ahead(1)
                    dve.wait_ge(f.h_hi_ready, 2 * i + t + 1)
                    dve.tensor_tensor(h_lo[:, 2 * i + t, :], tmp[:, t, :], f32(h_hi[:, 2 * i + t, :]),
                                      ALU.subtract).then_inc(f.h_ready, 1)

                with dve.Fori(0, FT // 2 - 1) as i:
                    for t in range(2):
                        tile(t, i, lambda s: lo(f.base + RING + 2 * t + s, i))
                last = FT // 2 - 1
                for t in range(2):
                    tile(t, last, lambda s: lo(f.base + RING + 2 * t + s + RING * last))
                for j in range(DT):
                    n = f.base + U_IN + 3 * j + RING
                    lo(n)
                    lo(n + 1)
                    dve.wait_ge(unit_used, f.base + U_IN + 3 * j + 3)
                    dve.scalar_tensor_tensor(halves(x[:, j, :]), pair(2 * (j % 2)), 0.5,
                                             halves(x[:, j, :]), ALU.mult, ALU.add).then_inc(x_ready, 1)
                    if next_norm is not None:
                        u_low(j, next_norm, next_u + j + 1)
                    lo(n + 2)

            lo(0)
            dve.wait_ge(gains_landed, 16)
            for j in range(DT):
                dve.wait_ge(x_landed[j], 16)
                u_low(j, 0, j + 1)
                if j in FIRST_UNITS:
                    lo(FIRST_UNITS.index(j) + 1)
            dve.wait_ge(consts_landed, 64)
            dve.wait_ge(hist_hi, 1)
            dve.tensor_tensor(u_lo[:, :, TOK:TOK + HIST], hist[:, :, :], f32(u_hi[:, :, TOK:TOK + HIST]),
                              ALU.subtract).then_inc(hist_lo, 1)
            dve.tensor_tensor(pool_bs[:, :], vecs[:, 0, :], vecs[:, 1, :], ALU.mult) \
                .then_inc(x_ready, DT)
            ffn(ffn_a, N_POOL, 8)

            rstd_cols(N_POOL, 4 + 2 * HIST)

            def pool_x(g):
                for m in range(2):
                    j = 2 * g + m
                    dve.wait_ge(pool_y_ready, j + 1)
                    if j == 0:
                        dve.wait_ge(state_made, 1)
                    dve.tensor_tensor(x[:, j, :], x[:, j, :], pool_y[:, m, :], ALU.add).then_inc(x_ready, 1)
                for m in range(2):
                    u_low(2 * g + m, 2, 2 * DT + 2 * g + m + 1)
                lo(U_B + g)

            for g in range(GROUPS):
                dve.wait_ge(unit_used, U_POOL + g + 1)
                for c in range(2):
                    last = dve.tensor_scalar(z[:, g, c, :], z_place(g, c, P), rms_col[:, c:c + 1], None,
                                             ALU.mult)
                last.then_inc(z_dve, 1)
                if g >= 2:
                    pool_x(g - 2)
            pool_x(GROUPS - 2)
            pool_x(GROUPS - 1)
            ffn(ffn_b, 3, 24)
            ffn(ffn_c, 4, 32)

            rstd_of(N_MIX)
            dve.wait_ge(unit_used, U_M + 1)
            dve.tensor_tensor(halves(r_f[:, :]), ps[32:36, 4:6, 0:HALF], halves(rstd[32:36, :]), ALU.mult) \
                .then_inc(proj_read, 1)
            last = dve.tensor_tensor(halves(r_a[:, :]), ps[0:4, 4:6, 0:HALF], halves(rstd[0:4, :]), ALU.mult)
            last.then_inc(proj_read, 1)
            dve.wait_ge(proj_read, 2)
            link(dve.tensor_scalar(r_f[:, :], r_f[:, :], gate_b[:, 1:2], None, ALU.add))
            dve.tensor_scalar(r_a[:, :], r_a[:, :], gate_b[:, 0:1], None, ALU.add)
            dve.scalar_tensor_tensor(r_e[:, :], r_f[:, :], -1.0, r_f[:, :], ALU.mult, ALU.max) \
                .then_inc(gate_abs, 1)
            lo(U_M + RING)
            for g in range(1, 9):
                dve.wait_ge(unit_used, U_M + g + 1)
                b = 2 * (g % 2)
                if g <= 4:
                    dve.scalar_tensor_tensor(halves(q_t[:, g - 1, :]), pair(b), float(P) ** -0.5,
                                             halves(rstd[:, :]), ALU.mult, ALU.mult).then_inc(proj_read, 1)
                else:
                    scaled(k_t[:, g - 5, :], b).then_inc(proj_read, 1)
                if g == 2:
                    dve.wait_ge(gate_log, 1)
                    link(dve.scalar_tensor_tensor(r_f[:, :], r_f[:, :], 0.0, r_e[:, :], ALU.min, ALU.subtract))
                    dve.tensor_tensor_scan(r_e[:, 0:SEQ], r_f[:, 0:SEQ], r_f[:, 0:SEQ], 0.0, ALU.add, ALU.min)
                    link(dve.tensor_tensor_scan(r_e[:, SEQ:TOK], r_f[:, SEQ:TOK], r_f[:, SEQ:TOK], 0.0,
                                                ALU.add, ALU.min))
                if g == 3:
                    link(dve.tensor_tensor(r_a[:, :], r_a[:, :], r_e[:, :], ALU.subtract))
                    dve.tensor_tensor_scan(r_m[:, 0:SEQ], r_a[:, 0:SEQ], r_a[:, 0:SEQ], 0.0, ALU.max, ALU.max)
                    link(dve.tensor_tensor_scan(r_m[:, SEQ:TOK], r_a[:, SEQ:TOK], r_a[:, SEQ:TOK],
                                                m_first[:, :], ALU.max, ALU.max))
                    dve.tensor_tensor(r_f[:, :], r_e[:, :], r_m[:, :], ALU.add).then_inc(rows_ready, 1)
                lo(U_M + RING + g)

            def item(kind, n, k):
                b = 4 + 2 * (k % 2)
                if kind == "cols":
                    dve.wait_ge(core_psum, k + 1)
                    dve.tensor_copy(cols[:, 0:36], ps[:, b, 0:36])
                    dve.tensor_copy(cols[0:DEC_SEQ, 36:44], ps[0:DEC_SEQ, b, 36:44]).then_inc(dve_took, 1)
                elif kind == "mb" and n == HEADS - 1:
                    dve.wait_ge(*taken(k))
                    dve.tensor_copy(mend[:, 0:4, :], m_b[:, :, CH - 1:SEQ:CH].transpose([0, 2, 1]))
                    dve.tensor_copy(mend[:, 4, :], cols[:, 32:36])
                    link(dve.tensor_copy(mend[:, 5, :], m_b[:, :, TOK - 1]))
                    dve.tensor_tensor(w_write[:, 0:4, :], cols[:, 0:16].rearrange("p (c h) -> p c h", c=4),
                                      mend[:, 0:4, :], ALU.subtract)
                    dve.tensor_tensor(w_write[0:DEC_SEQ, 4, :], cols[0:DEC_SEQ, 36:40], mend[0:DEC_SEQ, 5, :],
                                      ALU.subtract)
                    dve.tensor_tensor(carry[:, 0:3, :], mend[:, 0:3, :], mend[:, 1:4, :], ALU.subtract)
                    dve.tensor_tensor(carry[:, 3, :], mend[:, 4, :], mend[:, 5, :], ALU.subtract) \
                        .then_inc(ends_ready, 1)
                elif kind == "sk":
                    if n == 0:
                        dve.wait_ge(sel_made, 3)
                    c0, L = block_cols(n)
                    a0 = 4 * n if n < NB - 1 else 36
                    for h in range(HEADS):
                        last = dve.scalar_tensor_tensor(probs[0:L, h, c0:c0 + L], m_b[0:L, h, c0:c0 + L],
                                                        cols[0:L, a0 + h:a0 + h + 1], later[0:L, 0:L],
                                                        ALU.subtract, ALU.max)
                    last.then_inc(expo_ready, 1)
                    dve.wait_ge(factors_ready, 1)
                    dve.wait_ge(core_psum, k + 1)
                    dve.tensor_tensor(k_w[0:L, n, :, :], ps[0:L, b + 1, :].rearrange("p (h d) -> p h d", h=4),
                                      w_write[0:L, n, :].unsqueeze(2).to_broadcast([L, HEADS, P]), ALU.mult)
                    dve.wait_ge(expo_done, n + 1)
                    dve.tensor_tensor(probs[0:L, :, c0:c0 + L], probs[0:L, :, c0:c0 + L],
                                      ps[0:L, b, 0:HEADS * L].rearrange("p (h t) -> p h t", h=HEADS),
                                      ALU.mult).then_inc(dve_took, 1)
                    if n >= 1:
                        dve.wait_ge(q_factor, n)
                        dve.tensor_tensor(q_t[:, :, c0:c0 + L], q_t[:, :, c0:c0 + L], m_b[:, :, c0:c0 + L],
                                          ALU.mult).then_inc(q_scaled, 1)

            for t in range(DT):
                dve.wait_ge(unit_used, U_M + 9 + t + 1)
                scaled(og[:, t, :], 2 * ((9 + t) % 2)).then_inc(proj_read, 1)
                lo(U_M + RING + 9 + t)
                for k, (kind, n) in enumerate(AFTER_V[t], ITEM_AT[t]):
                    item(kind, n, k)

            def chunk(kind, c):
                _, L = block_cols(c)
                old, new = old_state(c)
                if kind == "upd":
                    dve.wait_ge(upd_psum, c + 1)
                    if c == 0:
                        dve.tensor_copy(c_st[:, new, :, :], ps[:, 4:8, 0:DV + 1]).then_inc(state_ready, 1)
                        return
                    if c == NB - 1:
                        dve.wait_ge(state_landed, 16)
                    else:
                        dve.wait_ge(state_ready, c)
                    for h in range(HEADS):
                        last = dve.scalar_tensor_tensor(
                            c_st[:, new, h, :], c_st[:, old, h, :],
                            carry[:, c - 1:c, h], ps[:, 4 + h, 0:DV + 1], ALU.mult, ALU.add)
                    last.then_inc(state_ready, 1)
                elif kind == "out":
                    dve.wait_ge(out_psum, c + 1)
                    dve.tensor_copy(v_one[0:L, c, :, :], ps[0:L, 4:8, 0:DV + 1]).then_inc(out_read, 1)

            def variance(r):
                first, end, L = ROUNDS[r]
                den = v_one[0:L, first:end, :, DV]
                d, v = dd[0:L, first:end, :], hv[0:L, first:end, :]
                e0 = 16 + 4 * first if first < NB - 1 else 40
                enm = cols[0:L, e0:e0 + 4 * (end - first)].rearrange("p (c h) -> p c h", h=HEADS)
                dve.wait_ge(squares, end)
                link(dve.scalar_tensor_tensor(d, den, -1.0, den, ALU.mult, ALU.max))
                link(dve.tensor_tensor(d, d, enm, ALU.max))
                link(dve.reciprocal(d, d))
                link(dve.tensor_tensor(v, d, d, ALU.mult))
                dve.tensor_tensor(v, v, ssum[0:L, first:end, :], ALU.mult).then_inc(var_ready, 1)

            def head_scale(r):
                first, end, L = ROUNDS[r]
                d, v = dd[0:L, first:end, :], hv[0:L, first:end, :]
                dve.wait_ge(root_done, r + 1)
                link(dve.reciprocal(v, v))
                dve.tensor_tensor(d, d, v, ALU.mult).then_inc(scale_ready, 1)

            for j in range(DT):
                middle, behind = IN_O[j]
                if middle and middle[0] == "out":
                    chunk(*middle)
                dve.wait_ge(unit_used, U_M + 17 + j + 1)
                scaled(og[:, j, :], 2 * ((17 + j) % 2)).then_inc(proj_read, 1)
                lo(U_M + RING + 17 + j)
                if behind:
                    chunk(*behind)
                if j in BEFORE_ROOT:
                    variance(BEFORE_ROOT.index(j))
                if j - 1 in BEFORE_ROOT:
                    head_scale(BEFORE_ROOT.index(j - 1))

            def y_low(j):
                dve.wait_ge(y_hi, j + 1)
                dve.tensor_tensor(u_lo[:, j, 0:TOK], tmp[:, j % 2, :], f32(u_hi[:, j, 0:TOK]), ALU.subtract) \
                    .then_inc(y_lo, 1)

            dve.wait_ge(m_out_done, 32)
            for j in range(DT):
                b = 4 + 2 * (j % 2)
                dve.wait_ge(y_psum, j + 1)
                dve.wait_ge(og_ready, j + 1)
                if j >= 2:
                    dve.wait_ge(y_lo, j - 1)
                dve.scalar_tensor_tensor(tmp[:, j % 2, 0:SEQ], ps[:, b, :], vecs[:, 2, j:j + 1],
                                         og[:, j, 0:SEQ], ALU.mult, ALU.mult)
                dve.scalar_tensor_tensor(tmp[:, j % 2, SEQ:TOK], ps[:, b + 1, 0:DEC_SEQ], vecs[:, 2, j:j + 1],
                                         og[:, j, SEQ:TOK], ALU.mult, ALU.mult).then_inc(y_read, 1)
                if j >= 1:
                    y_low(j - 1)
            y_low(DT - 1)
            for j in range(DT):
                if j == DT - 1:
                    for jj in range(DT - 2):
                        u_low(jj, 5, 5 * DT + jj + 1)
                dve.wait_ge(unit_used, U_MOUT + j + 1)
                dve.tensor_tensor(halves(x[:, j, :]), halves(x[:, j, :]), pair(2 * (j % 2)), ALU.add) \
                    .then_inc(x_ready, 1)
                if j < DT - 1:
                    lo(U_MOUT + RING + j)
            for j in (DT - 2, DT - 1):
                u_low(j, 5, 5 * DT + j + 1)
            lo(U_MOUT + RING + DT - 1)
            ffn(ffn_d, None, 0)

            rstd_cols(N_FINAL, 4)
            for c in range(NB):
                _, L = block_cols(c)
                col = c if c < NB - 1 else SAMPLE_COL
                dve.tensor_scalar(diag[0:L, c, 0:L], ident[0:L, 0:L], rms_col[0:L, col:col + 1],
                                  float(D_MODEL), ALU.mult, ALU.mult).then_inc(diag_ready, 1)
            dve.wait_ge(rstd_copied, 1)
            for j in range(N_POOL_OUT, DT):
                dve.scalar_tensor_tensor(x[:, j, :], x[:, j, :], gains[:, N_FINAL, j:j + 1], rstd[:, :],
                                         ALU.mult, ALU.mult).then_inc(out_tile, 1)

        @block.tensor
        def _(pe):
            def block_mm(n, kk, k, bank, first, last):
                w_h, w_l = (w[:, n % RING, kk * P:(kk + 1) * P] for w in (w_hi, w_lo))
                m_h, m_l = k
                for p, (w, m) in enumerate(((w_h, m_h), (w_h, m_l), (w_l, m_h))):
                    for h in range(2):
                        mm = pe.matmul(ps[:, bank + h, 0:HALF], w, m[:, h * HALF:(h + 1) * HALF],
                                       start=first and p == 0, stop=last and p == 2)
                return mm

            def u_tile(k):
                return u_hi[:, k, :], u_lo[:, k, :]

            def project(n, bank, i=0, ready=None, base=0, middle=None, each=None):
                pe.wait_ge(lo_split, n + 1 + RING * i)
                for k in range(DT):
                    if ready is not None:
                        pe.wait_ge(ready, base + k + 1)
                    mm = block_mm(n, k, u_tile(k), bank, k == 0, k == DT - 1)
                    if k == DT - 1:
                        mm.then_inc(unit_used, 1)
                    elif each is not None:
                        mm.then_inc(each, 1)
                    if k == 3 and middle:
                        middle()

            def norm(n):
                pe.wait_ge(sumsq_ready, n + 1)
                for h in range(2):
                    mm = pe.matmul(ps[:, 6 + h, 0:HALF], mean_w[:, :], sumsq[:, h * HALF:(h + 1) * HALF],
                                   start=True, stop=True)
                mm.then_inc(norm_psum, 1)

            def norm_cols(n):
                pe.wait_ge(sumsq_ready, n + 1)
                pe.wait_ge(sq_last, {N_POOL: 1, N_FINAL: 2}[n])
                for c in range(NB):
                    c0, L = block_cols(c)
                    col = c if c < NB - 1 else SAMPLE_COL
                    pe.matmul(ps[0:L, 5, col:col + 1], sumsq[:, c0:c0 + L], mean_w[:, 0:1],
                              start=True, stop=False)
                    mm = pe.matmul(ps[0:L, 5, col:col + 1], sq[:, c0:c0 + L], mean_w[:, 0:1],
                                   start=False, stop=True)
                if n == N_POOL:
                    for s, end in enumerate((SEQ, TOK)):
                        at = ps[:, 5, 4 + HIST * s:4 + HIST * (s + 1)]
                        pe.matmul(at, mean_w[:, :], sumsq[:, end - HIST:end], start=True, stop=False)
                        mm = pe.matmul(at, mean_w[:, :], sq[:, end - HIST:end], start=False, stop=True)
                mm.then_inc(norm_psum, 1)

            def project_two(n, bank, ready, base, ahead=None):
                for k in range(DT):
                    if ahead:
                        ahead(k)
                    pe.wait_ge(ready, base + k + 1)
                    for s in range(2):
                        if k == 0:
                            pe.wait_ge(lo_split, n + s + 1)
                        mm = block_mm(n + s, k, u_tile(k), bank + 2 * s, k == 0, k == DT - 1)
                        if k == DT - 1:
                            mm.then_inc(unit_used, 1)

            def ffn(f):
                if f is ffn_a:
                    project_two(f.base, 0, u_ready, f.u_base)
                    project(f.base + 2, 4)
                    norm(f.norm)
                elif f is ffn_b:
                    project_two(f.base, 0, u_ready, f.u_base)
                    norm(f.norm)
                    project(f.base + 2, 4)
                else:
                    pe.wait_ge(x_ready, DT * (f.norm + 1) - 1)
                    project(f.base, 0, ready=u_ready, base=f.u_base)
                    norm(f.norm)
                    pe.wait_ge(x_ready, DT * (f.norm + 1))
                    project(f.base + 1, 2)
                    project(f.base + 2, 4)
                pe.wait_ge(norm_root, f.norm + 1)
                project(f.base + 3, 6)
                with pe.Fori(1, FT // 2) as i:
                    for t in range(2):
                        pe.wait_ge(f.psum_read, 2 * i + t - 1)
                        project(f.base + 2 * t, 4 * t, i)
                        project(f.base + 2 * t + 1, 4 * t + 2, i)
                with pe.Fori(0, DT // 4) as i:
                    for jj in range(4):
                        pe.wait_ge(f.psum_read, FT - 1)
                        pe.wait_ge(x_ready, DT * (f.norm + 1) + (4 * i + jj - 1 if jj else 3 * i))
                        k = 0
                        for s, size in enumerate(OUT_UNIT):
                            n = f.base + U_IN + 3 * jj + s
                            pe.wait_ge(lo_split, n + 1 + 3 * 4 * i)
                            for kk in range(size):
                                if jj == 0:
                                    pe.wait_ge(f.h_ready, k + 1)
                                mm = block_mm(n, kk, (h_hi[:, k, :], h_lo[:, k, :]), 2 * (jj % 2),
                                              k == 0, k == FT - 1)
                                k += 1
                            mm.then_inc(unit_used, 1)

            pe.wait_ge(mean_made, 1)
            for _ in range(18):
                pe.matmul(ps[:, 7, 0:P], mean_w[:, :], mean_w[:, :], start=True, stop=True)
            pe.wait_ge(consts_made, 2)
            ffn(ffn_a)

            def pool_project(g):
                pe.wait_ge(lo_split, U_POOL + g + 1)
                pe.wait_ge(u_ready, DT + 2 * g + 2)
                w_h, w_l = (w[:, (U_POOL + g) % RING, :] for w in (w_hi, w_lo))
                if g >= 2:
                    pe.wait_ge(z_dve, g - 1)
                    pe.wait_ge(z_act, g - 1)
                for c in range(NB):
                    if g == 0 and c == NB - 1:
                        pe.wait_ge(x_ready, 2 * DT)
                    elif c == NB - 1:
                        pe.wait_ge(z_act, g)
                    c0, L = block_cols(c)
                    if c == NB - 1:
                        L += HIST
                    for k in range(2):
                        u_h, u_l = (u[:, 2 * g + k, c0:c0 + L] for u in (u_hi, u_lo))
                        for p, (u, w) in enumerate(((u_h, w_h), (u_h, w_l), (u_l, w_h))):
                            mm = pe.matmul(z_place(g, c, L), u, w[:, 2 * P * k:2 * P * (k + 1)],
                                           start=k == 0 and p == 0, stop=k == 1 and p == 2)
                mm.then_inc(unit_used, 1)

            def pool_windows(g):
                pe.wait_ge(z_dve, g + 1)
                pe.wait_ge(z_act, g + 1)
                for m in range(2):
                    j = 2 * g + m
                    zs = [z[:, g, c, m * P:(m + 1) * P] for c in range(NB - 1)]
                    pe.matmul(ps[:, 6 + m, 0:HIST], zs[0], bands[:, g, START:LAST], start=True, stop=True)
                    pe.matmul(ps[:, 6 + m, HIST:CH], zs[0], bands[:, g, IN + HIST:NEXT], start=True, stop=True)
                    for c in range(1, NB - 1):
                        pe.matmul(ps[:, 6 + m, c * CH:(c + 1) * CH], zs[c], bands[:, g, IN:NEXT],
                                  start=True, stop=False)
                        pe.matmul(ps[:, 6 + m, c * CH:c * CH + HIST], zs[c - 1], bands[:, g, NEXT:START],
                                  start=False, stop=True)
                    rows = DEC_SEQ + HIST
                    if j:
                        pe.wait_ge(pool_y_ready, j)
                    pe.matmul(ps[:, 5, 0:DEC_SEQ], z[0:rows, g, NB - 1, m * P:(m + 1) * P],
                              bands[0:rows, g, LAST:BAND], start=True, stop=True).then_inc(pool_psum, 1)

            pe.wait_ge(x_ready, 2 * DT - 1)
            pe.wait_ge(hist_lo, 1)
            pool_project(0)
            norm_cols(N_POOL)
            pool_project(1)
            pool_project(2)
            pe.wait_ge(bands_landed, 16)
            pool_windows(0)
            pool_project(3)
            for g in range(1, GROUPS):
                pool_windows(g)
            ffn(ffn_b)
            ffn(ffn_c)

            project(U_M, 4, ready=u_ready, base=4 * DT)
            norm(N_MIX)
            pe.wait_ge(x_ready, 5 * DT)
            for g in range(1, 9):
                if g > 2:
                    pe.wait_ge(proj_read, g)
                project(U_M + g, 2 * (g % 2))

            def item(kind, n, k):
                b = 4 + 2 * (k % 2)
                if k >= 2:
                    pe.wait_ge(*taken(k - 2))
                if k == 1:
                    pe.wait_ge(norm_root, N_MIX + 1)
                if kind == "cols":
                    pe.wait_ge(enm_row, 1)
                    pe.wait_ge(sel_made, 3)
                    for c in range(NB):
                        c0, L = block_cols(c)
                        for r, rows in enumerate((r_a, r_e)):
                            o = 16 * r + 4 * c if c < NB - 1 else 36 + 4 * r
                            pe.matmul(ps[0:L, b, o:o + 4], rows[:, c0:c0 + L], ident[0:4, 0:4],
                                      start=True, stop=True)
                    for h in range(HEADS):
                        mm = pe.matmul(ps[:, b, 32 + h:33 + h], sel[:, h, :], m_first[:, :],
                                       start=True, stop=True)
                elif kind == "mb":
                    for h in range(2):
                        mm = pe.matmul(ps[:, b + h, 0:HALF], sel[:, n, :], r_m[:, h * HALF:(h + 1) * HALF],
                                       start=True, stop=True)
                elif kind == "vt":
                    pe.wait_ge(proj_read, 10 + n + 1)
                    for c in range(NB - 1):
                        pe.transpose(ps[:, b, c * CH:(c + 1) * CH], og[:, n, c * CH:(c + 1) * CH], ident[:, :])
                    mm = pe.matmul(ps[0:DEC_SEQ, b + 1, 0:P], og[:, n, SEQ:TOK], ident[:, :],
                                   start=True, stop=True)
                elif kind == "sk":
                    c0, L = block_cols(n)
                    for h in range(HEADS):
                        k_c = k_t[:, h, c0:c0 + L]
                        pe.matmul(ps[0:L, b, h * L:(h + 1) * L], k_c, q_t[:, h, c0:c0 + L],
                                  start=True, stop=True)
                        if L == P:
                            mm = pe.transpose(ps[:, b + 1, h * P:(h + 1) * P], k_c, ident[:, :])
                        else:
                            mm = pe.matmul(ps[0:L, b + 1, h * P:(h + 1) * P], k_c, ident[:, :],
                                           start=True, stop=True)
                mm.then_inc(core_psum, 1)

            def chunk(kind, c):
                c0, L = block_cols(c)
                old, _ = old_state(c)
                if kind == "upd":
                    if c == 0:
                        pe.wait_ge(*taken(ITEM_AT[9] - 2))
                        pe.wait_ge(*taken(ITEM_AT[9] - 1))
                    else:
                        pe.wait_ge(out_read, c)
                    for h in range(HEADS):
                        mm = pe.matmul(ps[:, 4 + h, 0:DV + 1], k_w[0:L, c, h, :], v_one[0:L, c, h, :],
                                       start=True, stop=True)
                    mm.then_inc(upd_psum, 1)
                else:
                    pe.wait_ge(state_ready, c + 1)
                    if c:
                        pe.wait_ge(q_scaled, c)
                    if c == NB - 1:
                        pe.wait_ge(state_landed, 16)
                    for h in range(HEADS):
                        mm = pe.matmul(ps[0:L, 4 + h, 0:DV + 1], probs[0:L, h, c0:c0 + L],
                                       v_one[0:L, c, h, :], start=True, stop=c == 0)
                        if c:
                            mm = pe.matmul(ps[0:L, 4 + h, 0:DV + 1], q_t[:, h, c0:c0 + L],
                                           c_st[:, old, h, :], start=False, stop=True)
                    mm.then_inc(out_psum, 1)

            for t in range(DT):
                pe.wait_ge(proj_read, 9 + t)
                project(U_M + 9 + t, 2 * ((9 + t) % 2))
                for k, (kind, n) in enumerate(AFTER_V[t], ITEM_AT[t]):
                    item(kind, n, k)

            def in_o(what):
                if what and what[0] == "vt":
                    item("vt", 7, ITEM_AT[8])
                elif what:
                    chunk(*what)

            for j in range(DT):
                pe.wait_ge(proj_read, 17 + j)
                middle, behind = IN_O[j]
                project(U_M + 17 + j, 2 * ((17 + j) % 2), middle=lambda: in_o(middle))
                in_o(behind)
            pe.wait_ge(h_scaled, NB)

            def heads_back(j):
                b = 4 + 2 * (j % 2)
                h, d0 = j // 2, j % 2 * P
                if j >= 2:
                    pe.wait_ge(y_read, j - 1)
                for c in range(NB - 1):
                    pe.transpose(ps[:, b, c * CH:(c + 1) * CH], v_one[:, c, h, d0:d0 + P], ident[:, :])
                pe.matmul(ps[:, b + 1, 0:DEC_SEQ], v_one[0:DEC_SEQ, NB - 1, h, d0:d0 + P],
                          ident[0:DEC_SEQ, 0:DEC_SEQ], start=True, stop=True).then_inc(y_psum, 1)

            heads_back(0)
            heads_back(1)
            pe.wait_ge(proj_read, 26)
            project_two(U_MOUT, 0, y_lo, 0, ahead=lambda k: heads_back(k + 2) if k + 2 < DT else None)
            for j in range(2, DT):
                pe.wait_ge(x_ready, 5 * DT + j - 1)
                project(U_MOUT + j, 2 * (j % 2), each=u_free if j == DT - 1 else None)
            ffn(ffn_d)
            norm_cols(N_FINAL)
            for c in range(NB):
                c0, L = block_cols(c)
                pe.wait_ge(diag_ready, c + 1)
                t = c0
                while t < c0 + L:
                    h = t // HALF
                    e = min(c0 + L, (h + 1) * HALF)
                    mm = pe.matmul(ps[:, 6 + h, t - h * HALF:e - h * HALF], mean_w[0:L, :],
                                   diag[0:L, c, t - c0:e - c0], start=True, stop=True)
                    t = e
            mm.then_inc(spread, 1)


def _tiles(v):
    return v.reshape((DT, P) + v.shape[1:]).swapaxes(0, 1)


def _bands():
    import numpy as np
    bands = np.zeros((P, GROUPS, BAND), np.float32)
    for g in range(GROUPS):
        w = 2 << g
        s, t = np.arange(P)[:, None], np.arange(P)[None, :]
        inside = (s <= t) & (s > t - w)
        bands[:, g, IN:NEXT] = inside / w - (s == t)
        bands[:, g, NEXT:START] = (s > P + t[:, :HIST] - w) / w
        bands[:, g, START:LAST] = (inside / np.minimum(t + 1, w) - (s == t))[:, :HIST]
        bands[:DEC_SEQ, g, LAST:BAND] = bands[:DEC_SEQ, g, IN:IN + DEC_SEQ]
        past = np.arange(-HIST, 0)[:, None]
        bands[DEC_SEQ:DEC_SEQ + HIST, g, LAST:BAND] = (past > t[:, :DEC_SEQ] - w) / w
    return bands


def kernel(x_prompt, x_sample, state_pool, state_mlstm_C, state_mlstm_n, state_mlstm_m, norm_ffn1,
           ffn1_w_in, ffn1_w_out, norm_mix, pool_w, pool_b, pool_scale, mlstm_w_in, mlstm_b_i, mlstm_b_f,
           mlstm_norm, mlstm_w_out, norm_ffn2, ffn2_w_in, ffn2_w_out, norm_final):
    import numpy as np
    import concourse.bacc as bacc
    from concourse.bass_utils import run_bass_kernel_spmd

    def ffn_in(w):
        return np.asarray(w).reshape(2, DT, P, 2, FT, P).transpose(0, 4, 3, 2, 1, 5).reshape(2, 2 * FT, P, DT * P)

    def ffn_out(w):
        return np.asarray(w).reshape(2, FT, P, DT, P).transpose(0, 3, 2, 1, 4).reshape(2, DT, P, FT * P)

    def square_w(w, n):
        return np.asarray(w).reshape(DT, P, n, P).transpose(2, 1, 0, 3).reshape(n, P, DT * P)

    w_mix = np.asarray(mlstm_w_in)[0]
    f1, mx, f2 = np.asarray(norm_ffn1), np.asarray(norm_mix), np.asarray(norm_ffn2)
    gains = np.stack([f1[0], mx[0], f2[0], f1[1], mx[1], f2[1], np.asarray(norm_final)], 1)
    vecs = np.stack([np.asarray(v)[0] for v in (pool_b, pool_scale, mlstm_norm)], 1)
    ins = {
        "x": _tiles(np.concatenate([np.asarray(x_prompt)[0], np.asarray(x_sample)[0]]).T),
        "pool_hist": _tiles(np.asarray(state_pool)[0, 0].T),
        "bands": _bands(),
        "state_c": np.concatenate([np.asarray(state_mlstm_C)[0, 0].transpose(2, 0, 1),
                                   np.asarray(state_mlstm_n)[0, 0].T[:, :, None]], 2),
        "state_m": np.asarray(state_mlstm_m)[0, 0].reshape(HEADS, 1),
        "gains": _tiles(gains).transpose(0, 2, 1),
        "vecs": _tiles(vecs).transpose(0, 2, 1),
        "gate_b": np.stack([np.asarray(mlstm_b_i)[0], np.asarray(mlstm_b_f)[0]], 1),
        "ffn1_in": ffn_in(ffn1_w_in), "ffn1_out": ffn_out(ffn1_w_out),
        "ffn2_in": ffn_in(ffn2_w_in), "ffn2_out": ffn_out(ffn2_w_out),
        "pool_w": np.asarray(pool_w)[0].reshape(GROUPS, 2, P, 2 * P).transpose(0, 2, 1, 3).reshape(GROUPS, P, 4 * P),
        "mlstm_in": square_w(w_mix[:, :N_PROJ * P], N_PROJ),
        "mlstm_gates": _tiles(w_mix[:, N_PROJ * P:]).reshape(P, DT * 2 * HEADS),
        "mlstm_out": square_w(np.asarray(mlstm_w_out)[0], DT),
    }
    outs = {
        "y": (P, DT, TOK),
        "pool_prompt": (P, DT, HIST), "pool_sample": (P, DT, HIST),
        "c_prompt": (P, HEADS, DV + 1), "c_sample": (P, HEADS, DV + 1),
        "m_prompt": (HEADS, 1), "m_sample": (HEADS, 1),
    }
    nc = bacc.Bacc("TRN2", target_bir_lowering=False, num_devices=1)
    arrays, aps = {}, {}
    for name, v in ins.items():
        arrays["in_" + name] = np.ascontiguousarray(v)
        aps[name] = nc.dram_tensor("in_" + name, v.shape, mybir.dt.from_np(v.dtype), kind="ExternalInput").ap()
    for name, shape in outs.items():
        aps[name] = nc.dram_tensor("out_" + name, shape, mybir.dt.float32, kind="ExternalOutput").ap()
    encoder_step(nc, aps)
    got = run_bass_kernel_spmd(nc, [arrays], core_ids=[0]).results[0]
    r = {name: got["out_" + name] for name in outs}

    def rows(v):
        return np.ascontiguousarray(v.transpose(2, 1, 0).reshape(1, v.shape[2], D_MODEL))

    def state(v):
        return (np.ascontiguousarray(v[:, :, :DV].transpose(1, 2, 0))[None, None],
                np.ascontiguousarray(v[:, :, DV].T)[None, None])

    c_p, n_p = state(r["c_prompt"])
    c_s, n_s = state(r["c_sample"])
    return (rows(r["y"][:, :, :SEQ]), rows(r["y"][:, :, SEQ:]), rows(r["pool_prompt"])[None], c_p, n_p,
            r["m_prompt"].reshape(1, 1, HEADS), rows(r["pool_sample"])[None], c_s, n_s,
            r["m_sample"].reshape(1, 1, HEADS))
```
